# Optimizing a Trainium2 kernel written in Bass

```python
import math
import jax, jax.numpy as jnp
from jax import lax
import numpy as np

D_MODEL = 1024
BATCH = 1
SEQ = 512
DEPTH = 1

HEAD_DIM = 64
N_DIFF_HEADS = 4
DIFF_V_DIM = 2 * HEAD_DIM
N_SB_HEADS = 8
DIFF_QK_WIDTH = N_DIFF_HEADS * 2 * HEAD_DIM
DIFF_V_WIDTH = N_DIFF_HEADS * DIFF_V_DIM
SB_WIDTH = N_SB_HEADS * HEAD_DIM
MIX_WIDTH = DIFF_V_WIDTH + SB_WIDTH
QKV_WIDTH = 2 * DIFF_QK_WIDTH + DIFF_V_WIDTH + 3 * SB_WIDTH
QKV_SPLITS = (DIFF_QK_WIDTH, 2 * DIFF_QK_WIDTH, 2 * DIFF_QK_WIDTH + DIFF_V_WIDTH,
              2 * DIFF_QK_WIDTH + DIFF_V_WIDTH + SB_WIDTH,
              2 * DIFF_QK_WIDTH + DIFF_V_WIDTH + 2 * SB_WIDTH)
D_FF = 2816
CONV_WIDTH = 3
N_BUCKETS = 32
MAX_DISTANCE = 128
Q_BLOCK = 128
RMS_EPS = 1e-6


def _rmsnorm(x, g):
    xf = x.astype(jnp.float32)
    y = xf * lax.rsqrt(jnp.mean(xf * xf, axis=-1, keepdims=True) + RMS_EPS)
    return (y * g.astype(jnp.float32)).astype(x.dtype)

def _lambda_init(layer):
    return 0.8 - 0.6 * math.exp(-0.3 * layer)

def _relative_bucket(rel):
    n = jnp.maximum(rel, 0)
    max_exact = N_BUCKETS // 2
    nf = jnp.maximum(n, 1).astype(jnp.float32)
    large = max_exact + (jnp.log(nf / max_exact) / math.log(MAX_DISTANCE / max_exact)
                         * (N_BUCKETS - max_exact)).astype(jnp.int32)
    large = jnp.minimum(large, N_BUCKETS - 1)
    return jnp.where(n < max_exact, n, large)

def _diff_attention(q, k, v, lam, rel_bias):
    B, H, _, S, d = q.shape
    nb = S // Q_BLOCK
    qb = q.reshape(B, H, 2, nb, Q_BLOCK, d).transpose(3, 0, 1, 2, 4, 5)
    starts = jnp.arange(nb, dtype=jnp.int32) * Q_BLOCK
    k_pos = jnp.arange(S, dtype=jnp.int32)
    scale = d ** -0.5
    table = rel_bias.astype(jnp.float32)

    def one_block(args):
        q_blk, t0 = args
        rel = (t0 + jnp.arange(Q_BLOCK, dtype=jnp.int32))[:, None] - k_pos[None, :]
        bias = jnp.transpose(table[_relative_bucket(rel)], (2, 0, 1))
        logits = jnp.einsum('bhmqd,bhmkd->bhmqk', q_blk, k).astype(jnp.float32) * scale
        logits = logits + bias[None, :, None]
        logits = jnp.where(rel >= 0, logits, -jnp.inf)
        p = jax.nn.softmax(logits, axis=-1)
        w = p[:, :, 0] - lam * p[:, :, 1]
        return jnp.einsum('bhqk,bhkd->bhqd', w.astype(v.dtype), v)

    out = lax.map(one_block, (qb, starts))
    return out.transpose(1, 2, 0, 3, 4).reshape(B, H, S, v.shape[-1])

def _stick_breaking_attention(q, k, v):
    B, H, S, d = q.shape
    nb = S // Q_BLOCK
    qb = q.reshape(B, H, nb, Q_BLOCK, d).transpose(2, 0, 1, 3, 4)
    starts = jnp.arange(nb, dtype=jnp.int32) * Q_BLOCK
    k_pos = jnp.arange(S, dtype=jnp.int32)
    scale = d ** -0.5

    def one_block(args):
        q_blk, t0 = args
        rel = (t0 + jnp.arange(Q_BLOCK, dtype=jnp.int32))[:, None] - k_pos[None, :]
        strict = rel > 0
        z = jnp.einsum('bhqd,bhkd->bhqk', q_blk, k).astype(jnp.float32) * scale
        log_beta = jax.nn.log_sigmoid(z)
        log_1mb = jnp.where(strict, jax.nn.log_sigmoid(-z), 0.0)
        between = lax.cumsum(log_1mb, axis=3, reverse=True) - log_1mb
        a = jnp.where(strict, jnp.exp(log_beta + between), 0.0)
        return jnp.einsum('bhqk,bhkd->bhqd', a.astype(v.dtype), v)

    out = lax.map(one_block, (qb, starts))
    return out.transpose(1, 2, 0, 3, 4).reshape(B, H, S, d)

def _causal_depthwise_conv(u, w, b):
    S = u.shape[1]
    up = jnp.pad(u, ((0, 0), (CONV_WIDTH - 1, 0), (0, 0)))
    y = b
    for i in range(CONV_WIDTH):
        y = y + up[:, i:i + S] * w[i]
    return y

def first_inputs(seed: int = 0) -> dict:
    key = jax.random.key(seed)
    ks = jax.random.split(key, 18)

    def nrm(k, shape, scale):
        return jax.random.normal(k, shape, jnp.float32) * scale

    def gain(k, shape):
        return 1.0 + 0.05 * jax.random.normal(k, shape, jnp.float32)

    return {
        'x': nrm(ks[0], (BATCH, SEQ, D_MODEL), 1.0),
        'attn_pre_norm': gain(ks[1], (DEPTH, D_MODEL)),
        'w_qkv': nrm(ks[2], (DEPTH, D_MODEL, QKV_WIDTH), D_MODEL ** -0.5),
        'lambda_q1': nrm(ks[3], (DEPTH, HEAD_DIM), 0.1),
        'lambda_k1': nrm(ks[4], (DEPTH, HEAD_DIM), 0.1),
        'lambda_q2': nrm(ks[5], (DEPTH, HEAD_DIM), 0.1),
        'lambda_k2': nrm(ks[6], (DEPTH, HEAD_DIM), 0.1),
        'diff_subln': gain(ks[7], (DEPTH, DIFF_V_DIM)),
        'sb_norm': gain(ks[8], (DEPTH, HEAD_DIM)),
        'rel_bias': nrm(ks[9], (N_BUCKETS, N_DIFF_HEADS), 0.5),
        'w_o': nrm(ks[10], (DEPTH, MIX_WIDTH, D_MODEL), MIX_WIDTH ** -0.5),
        'attn_post_norm': gain(ks[11], (DEPTH, D_MODEL)),
        'ffn_pre_norm': gain(ks[12], (DEPTH, D_MODEL)),
        'w_up': nrm(ks[13], (DEPTH, D_MODEL, 2 * D_FF), D_MODEL ** -0.5),
        'conv_w': nrm(ks[14], (DEPTH, CONV_WIDTH, 2 * D_FF), CONV_WIDTH ** -0.5),
        'conv_b': nrm(ks[15], (DEPTH, 2 * D_FF), 0.01),
        'w_down': nrm(ks[16], (DEPTH, D_FF, D_MODEL), D_FF ** -0.5),
        'ffn_post_norm': gain(ks[17], (DEPTH, D_MODEL)),
    }

def first_block(x, attn_pre_norm, w_qkv, lambda_q1, lambda_k1, lambda_q2, lambda_k2,
              diff_subln, sb_norm, rel_bias, w_o, attn_post_norm, ffn_pre_norm,
              w_up, conv_w, conv_b, w_down, ffn_post_norm):
    B, S, _ = x.shape
    for l in range(DEPTH):
        lam_init = _lambda_init(l)
        h = _rmsnorm(x, attn_pre_norm[l])
        qkv = h @ w_qkv[l]
        dq, dk, dv, sq, sk, sv = jnp.split(qkv, QKV_SPLITS, axis=-1)
        dq = dq.reshape(B, S, N_DIFF_HEADS, 2, HEAD_DIM).transpose(0, 2, 3, 1, 4)
        dk = dk.reshape(B, S, N_DIFF_HEADS, 2, HEAD_DIM).transpose(0, 2, 3, 1, 4)
        dv = dv.reshape(B, S, N_DIFF_HEADS, DIFF_V_DIM).transpose(0, 2, 1, 3)
        lam = (jnp.exp(jnp.sum(lambda_q1[l].astype(jnp.float32) * lambda_k1[l].astype(jnp.float32)))
               - jnp.exp(jnp.sum(lambda_q2[l].astype(jnp.float32) * lambda_k2[l].astype(jnp.float32)))
               + lam_init)
        diff_o = _diff_attention(dq, dk, dv, lam, rel_bias)
        diff_o = _rmsnorm(diff_o, diff_subln[l]) * (1.0 - lam_init)
        diff_o = diff_o.transpose(0, 2, 1, 3).reshape(B, S, DIFF_V_WIDTH)

        sq = sq.reshape(B, S, N_SB_HEADS, HEAD_DIM).transpose(0, 2, 1, 3)
        sk = sk.reshape(B, S, N_SB_HEADS, HEAD_DIM).transpose(0, 2, 1, 3)
        sv = sv.reshape(B, S, N_SB_HEADS, HEAD_DIM).transpose(0, 2, 1, 3)
        sb_o = _rmsnorm(_stick_breaking_attention(sq, sk, sv), sb_norm[l])
        sb_o = sb_o.transpose(0, 2, 1, 3).reshape(B, S, SB_WIDTH)

        mix = jnp.concatenate([diff_o, sb_o], axis=-1) @ w_o[l]
        x = x + _rmsnorm(mix, attn_post_norm[l])

        h = _rmsnorm(x, ffn_pre_norm[l])
        u = _causal_depthwise_conv(h @ w_up[l], conv_w[l], conv_b[l])
        gate, val = jnp.split(u, 2, axis=-1)
        y = (jax.nn.gelu(gate, approximate=True) * val) @ w_down[l]
        x = x + _rmsnorm(y, ffn_post_norm[l])
    return x


GRID_W = 64
CTX_LEN = 256
N_Q_HEADS = 8
N_KV_HEADS = 2
GROUP = N_Q_HEADS // N_KV_HEADS
WINDOW = 128
BLOCK = 128
ROPE_THETA = 10000.0
N_FOURIER_GROUPS = 4
FOURIER_GROUP_CH = 128
FOURIER_W = N_FOURIER_GROUPS * FOURIER_GROUP_CH
Q_W = N_Q_HEADS * HEAD_DIM
KV_W = N_KV_HEADS * HEAD_DIM
IN_W = Q_W + 2 * KV_W + FOURIER_W + 2 * D_MODEL
EPS = 1e-6
NEG = -1e30


def rmsnorm(x, g):
    xf = x.astype(jnp.float32)
    xf = xf * lax.rsqrt(jnp.mean(xf * xf, axis=-1, keepdims=True) + EPS)
    return xf.astype(x.dtype) * g

def modulate(h, shift, scale):
    return h * (1 + scale) + shift

def adaln(cvec, w_mod, b_mod):
    return jnp.split(jax.nn.silu(cvec) @ w_mod + b_mod, 6, axis=-1)

def axial_rope_tables(rows, dtype):
    row = jnp.repeat(jnp.arange(rows), GRID_W).astype(jnp.float32)
    col = jnp.tile(jnp.arange(GRID_W), rows).astype(jnp.float32)
    half = HEAD_DIM // 2
    inv_freq = ROPE_THETA ** (-jnp.arange(0, half, 2, dtype=jnp.float32) / half)
    ang_r = (row[:, None] * inv_freq)[:, None, :]
    ang_c = (col[:, None] * inv_freq)[:, None, :]
    return tuple(t.astype(dtype) for t in (jnp.cos(ang_r), jnp.sin(ang_r), jnp.cos(ang_c), jnp.sin(ang_c)))

def rotate(x, cos, sin):
    x1, x2 = jnp.split(x, 2, axis=-1)
    return jnp.concatenate([x1 * cos - x2 * sin, x2 * cos + x1 * sin], axis=-1)

def apply_axial_rope(x, tabs):
    cos_r, sin_r, cos_c, sin_c = tabs
    xr, xc = jnp.split(x, 2, axis=-1)
    return jnp.concatenate([rotate(xr, cos_r, sin_r), rotate(xc, cos_c, sin_c)], axis=-1)

def split_proj(p):
    o1 = Q_W
    o2 = o1 + KV_W
    o3 = o2 + KV_W
    o4 = o3 + FOURIER_W
    o5 = o4 + D_MODEL
    return p[..., :o1], p[..., o1:o2], p[..., o2:o3], p[..., o3:o4], p[..., o4:o5], p[..., o5:]

def banded_window_attention(q, k, v, k_ctx, v_ctx, sink):
    B, S = q.shape[:2]
    L = k_ctx.shape[1]
    nb = S // BLOCK
    scale = HEAD_DIM ** -0.5
    qb = q.reshape(B, nb, BLOCK, N_KV_HEADS, GROUP, HEAD_DIM)

    def band(t):
        tp = jnp.pad(t, ((0, 0), (BLOCK, BLOCK), (0, 0), (0, 0)))
        tp = tp.reshape(B, nb + 2, BLOCK, N_KV_HEADS, HEAD_DIM)
        return jnp.concatenate([tp[:, :-2], tp[:, 1:-1], tp[:, 2:]], axis=2)

    kw, vw = band(k), band(v)
    s_loc = jnp.einsum('bnqhgd,bnkhd->bnhgqk', qb, kw).astype(jnp.float32) * scale
    s_ctx = jnp.einsum('bnqhgd,blhd->bnhgql', qb, k_ctx).astype(jnp.float32) * scale
    qi = jnp.arange(BLOCK)[:, None]
    kj = jnp.arange(3 * BLOCK)[None, :]
    rel = kj - BLOCK - qi
    kpos = jnp.arange(nb)[:, None, None] * BLOCK + kj[None] - BLOCK
    valid = (jnp.abs(rel) <= WINDOW)[None] & (kpos >= 0) & (kpos < S)
    s_loc = jnp.where(valid[None, :, None, None], s_loc, NEG)
    sink_l = jnp.broadcast_to(sink.astype(jnp.float32).reshape(1, 1, N_KV_HEADS, GROUP, 1, 1),
                              s_loc.shape[:-1] + (1,))
    p = jax.nn.softmax(jnp.concatenate([s_loc, s_ctx, sink_l], axis=-1), axis=-1)
    p_loc = p[..., :3 * BLOCK].astype(v.dtype)
    p_ctx = p[..., 3 * BLOCK:3 * BLOCK + L].astype(v.dtype)
    o = (jnp.einsum('bnhgqk,bnkhd->bnqhgd', p_loc, vw)
         + jnp.einsum('bnhgql,blhd->bnqhgd', p_ctx, v_ctx))
    return o.reshape(B, S, Q_W)

def context_attention(q, k, v, sink):
    B, L = q.shape[:2]
    scale = HEAD_DIM ** -0.5
    qg = q.reshape(B, L, N_KV_HEADS, GROUP, HEAD_DIM)
    s = jnp.einsum('blhgd,bmhd->bhglm', qg, k).astype(jnp.float32) * scale
    sink_l = jnp.broadcast_to(sink.astype(jnp.float32).reshape(1, N_KV_HEADS, GROUP, 1, 1),
                              s.shape[:-1] + (1,))
    p = jax.nn.softmax(jnp.concatenate([s, sink_l], axis=-1), axis=-1)[..., :L].astype(v.dtype)
    o = jnp.einsum('bhglm,bmhd->blhgd', p, v)
    return o.reshape(B, L, Q_W)

def fourier_mix(f):
    B, S = f.shape[:2]
    fg = f.reshape(B, S, N_FOURIER_GROUPS, FOURIER_GROUP_CH).astype(jnp.float32)
    out = jnp.fft.fft2(fg, axes=(1, 3), norm='ortho').real
    return out.reshape(B, S, FOURIER_W).astype(f.dtype)

def merge_branches(attn_o, four_o, g_a, g_f, w_pa, w_pf, w_out):
    m = jax.nn.sigmoid(g_a) * (attn_o @ w_pa) + jax.nn.sigmoid(g_f) * (four_o @ w_pf)
    return m @ w_out

def conv_ffn(h, w_up, conv_w, conv_b, w_down):
    u, gate = jnp.split(h @ w_up, 2, axis=-1)
    up = jnp.pad(u, ((0, 0), (1, 1), (0, 0)))
    u = up[:, :-2] * conv_w[0] + up[:, 1:-1] * conv_w[1] + up[:, 2:] * conv_w[2] + conv_b
    return (jax.nn.silu(u) * gate) @ w_down

def second_inputs(seed: int = 0) -> dict:
    key = jax.random.key(seed)
    ks = jax.random.split(key, 19)
    f32 = jnp.float32
    D = D_MODEL

    def nrm(k, shape, s):
        return jax.random.normal(k, shape, f32) * s

    return {
        'x': nrm(ks[0], (BATCH, SEQ, D), 1.0),
        'c': nrm(ks[1], (BATCH, D), 1.0),
        'ctx': nrm(ks[2], (BATCH, CTX_LEN, D), 1.0),
        'c_ctx': nrm(ks[3], (D,), 1.0),
        'w_mod': nrm(ks[4], (DEPTH, D, 6 * D), 0.5 * D ** -0.5),
        'b_mod': nrm(ks[5], (DEPTH, 6 * D), 0.01),
        'g_pre1': 1.0 + nrm(ks[6], (DEPTH, D), 0.05),
        'g_post1': 1.0 + nrm(ks[7], (DEPTH, D), 0.05),
        'g_pre2': 1.0 + nrm(ks[8], (DEPTH, D), 0.05),
        'g_post2': 1.0 + nrm(ks[9], (DEPTH, D), 0.05),
        'w_in': nrm(ks[10], (DEPTH, D, IN_W), D ** -0.5),
        'sink': nrm(ks[11], (DEPTH, N_Q_HEADS), 0.5),
        'w_pa': nrm(ks[12], (DEPTH, Q_W, D), Q_W ** -0.5),
        'w_pf': nrm(ks[13], (DEPTH, FOURIER_W, D), FOURIER_W ** -0.5),
        'w_out': nrm(ks[14], (DEPTH, D, D), D ** -0.5),
        'w_up': nrm(ks[15], (DEPTH, D, 2 * D_FF), D ** -0.5),
        'conv_w': nrm(ks[16], (DEPTH, CONV_WIDTH, D_FF), CONV_WIDTH ** -0.5),
        'conv_b': nrm(ks[17], (DEPTH, D_FF), 0.01),
        'w_down': nrm(ks[18], (DEPTH, D_FF, D), D_FF ** -0.5),
    }

def second_block(x, c, ctx, c_ctx, w_mod, b_mod, g_pre1, g_post1, g_pre2, g_post2,
              w_in, sink, w_pa, w_pf, w_out, w_up, conv_w, conv_b, w_down):
    B, S, _ = x.shape
    L = ctx.shape[1]
    ROWS = S // GRID_W
    tabs = axial_rope_tables(ROWS, x.dtype)
    for l in range(DEPTH):
        last = l == DEPTH - 1
        sh1, sc1, gt1, sh2, sc2, gt2 = [m[:, None] for m in adaln(c, w_mod[l], b_mod[l])]
        csh1, csc1, cgt1, csh2, csc2, cgt2 = adaln(c_ctx, w_mod[l], b_mod[l])

        h = modulate(rmsnorm(x, g_pre1[l]), sh1, sc1)
        hc = modulate(rmsnorm(ctx, g_pre1[l]), csh1, csc1)
        q, k, v, f, g_a, g_f = split_proj(h @ w_in[l])
        q = apply_axial_rope(q.reshape(B, S, N_Q_HEADS, HEAD_DIM), tabs)
        k = apply_axial_rope(k.reshape(B, S, N_KV_HEADS, HEAD_DIM), tabs)
        v = v.reshape(B, S, N_KV_HEADS, HEAD_DIM)
        if last:
            pc = hc @ w_in[l, :, :Q_W + 2 * KV_W]
        else:
            pc = hc @ w_in[l]
        kc = pc[..., Q_W:Q_W + KV_W].reshape(B, L, N_KV_HEADS, HEAD_DIM)
        vc = pc[..., Q_W + KV_W:Q_W + 2 * KV_W].reshape(B, L, N_KV_HEADS, HEAD_DIM)

        attn = banded_window_attention(q, k, v, kc, vc, sink[l])
        y = merge_branches(attn, fourier_mix(f), g_a, g_f, w_pa[l], w_pf[l], w_out[l])
        x = x + gt1 * rmsnorm(y, g_post1[l])

        if not last:
            qc, _, _, fc, g_ac, g_fc = split_proj(pc)
            attn_c = context_attention(qc.reshape(B, L, N_Q_HEADS, HEAD_DIM), kc, vc, sink[l])
            yc = merge_branches(attn_c, fourier_mix(fc), g_ac, g_fc, w_pa[l], w_pf[l], w_out[l])
            ctx = ctx + cgt1 * rmsnorm(yc, g_post1[l])

        h2 = modulate(rmsnorm(x, g_pre2[l]), sh2, sc2)
        x = x + gt2 * rmsnorm(conv_ffn(h2, w_up[l], conv_w[l], conv_b[l], w_down[l]), g_post2[l])

        if not last:
            hc2 = modulate(rmsnorm(ctx, g_pre2[l]), csh2, csc2)
            ctx = ctx + cgt2 * rmsnorm(conv_ffn(hc2, w_up[l], conv_w[l], conv_b[l], w_down[l]), g_post2[l])
    return x


def setup_inputs(seed=0):
    out = dict(first_inputs(seed))
    for name, value in second_inputs(seed + 1).items():
        if name != "x":
            out[name + "_2"] = value
    return out


def reference(
    x, attn_pre_norm, w_qkv, lambda_q1, lambda_k1, lambda_q2, lambda_k2, diff_subln, sb_norm,
    rel_bias, w_o, attn_post_norm, ffn_pre_norm, w_up, conv_w, conv_b, w_down, ffn_post_norm,
    c_2, ctx_2, c_ctx_2, w_mod_2, b_mod_2, g_pre1_2, g_post1_2, g_pre2_2, g_post2_2, w_in_2,
    sink_2, w_pa_2, w_pf_2, w_out_2, w_up_2, conv_w_2, conv_b_2, w_down_2,
):
    x = first_block(
        x, attn_pre_norm, w_qkv, lambda_q1, lambda_k1, lambda_q2, lambda_k2, diff_subln,
        sb_norm, rel_bias, w_o, attn_post_norm, ffn_pre_norm, w_up, conv_w, conv_b, w_down,
        ffn_post_norm,
    )
    return second_block(
        x, c_2, ctx_2, c_ctx_2, w_mod_2, b_mod_2, g_pre1_2, g_post1_2, g_pre2_2, g_post2_2,
        w_in_2, sink_2, w_pa_2, w_pf_2, w_out_2, w_up_2, conv_w_2, conv_b_2, w_down_2,
    )


_drawn_inputs = setup_inputs


def setup_inputs(seed=0):
    import zlib

    import numpy as np

    out = dict(_drawn_inputs(seed))
    spreads = {}
    factors = {'lambda_q1': 3.856,
     'lambda_k1': 2.799,
     'lambda_q2': 23.482,
     'conv_b': 6.78,
     'ctx_2': 3.563,
     'b_mod_2': 6.204,
     'g_pre1_2': 6.377,
     'g_post1_2': 6.934,
     'g_pre2_2': 4.413,
     'g_post2_2': 6.575,
     'sink_2': 8.0,
     'conv_b_2': 42.199}
    for name, (base, spread) in spreads.items():
        noise = np.random.default_rng([zlib.crc32(name.encode()), seed]).standard_normal(out[name].shape)
        drawn = base * np.exp(spread * noise) if base else spread * noise
        out[name] = __import__('jax').numpy.asarray(drawn.astype(out[name].dtype))
    for name, factor in factors.items():
        out[name] = (out[name] * factor).astype(out[name].dtype)
    return out
```

```python
import math
from collections import namedtuple

import numpy as np

import concourse.bass as bass
from concourse import mybir


T = 512
D = 1024
NF = 22
EPS = 1e-6
LAM_INIT = 0.2
NEG = -1e30
ZCAP = 320.0
SBNEG = -1e5
LN_EXP_SET = 6

_COLS = [
    ("g_pre1", 8), ("g_post1", 8), ("g_pre2", 8), ("g_post2", 8), ("subln", 1), ("sbn", 1), ("lam", 4),
    ("table", 4), ("sink", 8), ("cw", 132), ("cb", 44), ("c", 16), ("bmod", 48),
    ("h_pre1", 8), ("h_post1", 8), ("h_pre2", 8), ("h_post2", 8), ("dw", 66), ("db", 22),
]
COL = {}
_at = 0
for _n, _w in _COLS:
    COL[_n] = (_at, _at + _w)
    _at += _w
NV = _at

_CC = [("ident", 128), ("ones", 128), ("tri", 128), ("blk", 128), ("sbmask", 512), ("mlow", 128), ("mhigh", 128),
       ("perm", 128), ("cc", 128), ("sc", 128)]
CCOL = {}
_at = 0
for _n, _w in _CC:
    CCOL[_n] = (_at, _at + _w)
    _at += _w
NC = _at


Token = namedtuple("Token", "sem value")


class Engine:

    def __init__(self, sem):
        self.sem, self.n, self.queue = sem, 0, []

    def op(self, fn, *after, tick=True):
        self.n += tick
        self.queue.append((fn, after, (self.sem, 1) if tick else None))
        return Token(self.sem, self.n) if tick else None

    def dma(self, fn, sem, *after):
        self.queue.append((fn, after, (sem, 16)))

    def run(self, eng):
        waited = {}
        for fn, after, inc in self.queue:
            need, todo = {}, list(after)
            while todo:
                t = todo.pop()
                if isinstance(t, Token):
                    need[t.sem.name] = (t.sem, max(t.value, need.get(t.sem.name, (None, 0))[1]))
                elif t is not None:
                    todo += t
            for name, (sem, value) in need.items():
                if waited.get(name, 0) < value:
                    eng.wait_ge(sem, value)
                    waited[name] = value
            ins = fn()
            if inc:
                ins.then_inc(*inc)


def build(nc, a, out):
    f32, f32r, bf16 = mybir.dt.float32, mybir.dt.float32r, mybir.dt.bfloat16
    ALU, ACT, AX = mybir.AluOpType, mybir.ActivationFunctionType, mybir.AxisListType
    V, S, G, E = nc.vector, nc.scalar, nc.gpsimd, nc.tensor

    base = (nc.sbuf_base + 31) // 32 * 32
    R = {}
    for name, size in [("H", 32768), ("A", 49152), ("M", 32768), ("X", 16384), ("RAW", 20480), ("HL", 40960),
                       ("G", 12288), ("K", 7744)]:
        R[name] = base
        base += size
    assert base <= nc.sbuf_usable_end, base

    def at(name, region, off, shape, dt=f32):
        return nc.alloc_sbuf_tensor_at(name, shape, dt, offset=R[region] + off).ap()

    Hhi = at("Hhi", "H", 0, [128, 8, T], f32r)
    Hlo = at("Hlo", "H", 16384, [128, 8, T], f32r)
    X = at("X", "X", 0, [128, 8, T])
    raw = [at(f"raw{i}", "RAW", 4096 * i, [128, 1024]) for i in range(5)]
    whi = [at(f"whi{i}", "HL", 8192 * i, [128, 1024], f32r) for i in range(5)]
    wlo = [at(f"wlo{i}", "HL", 8192 * i + 4096, [128, 1024], f32r) for i in range(5)]
    vec = at("vec", "K", 0, [128, NV])
    kk = (NV * 4 + 31) // 32 * 32
    ident = at("ident", "K", kk, [128, 128])
    ones = at("ones", "K", kk + 512, [128, 128])
    tri = at("tri", "K", kk + 1024, [128, 128])
    blk = at("blk", "K", kk + 1536, [128, 128])
    sbmask = at("sbmask", "K", kk + 2048, [128, 512])
    identb = at("identb", "K", kk + 4096, [128, 128], bf16)
    mlowb = at("mlowb", "K", kk + 4352, [128, 128], bf16)
    mhighb = at("mhighb", "K", kk + 4608, [128, 128], bf16)
    small = at("small", "K", kk + 4864, [128, 240])
    assert kk + 4864 + 960 <= 7744

    def vc(name, i=0, n=None):
        lo, hi = COL[name]
        return vec[:, lo + i:lo + i + 1] if n is None else vec[:, lo + i:lo + i + n]

    epsc, onec = small[:, 0:1], small[:, 1:2]
    lamc, gd = small[:, 2:3], small[:, 3:4]
    lprod, lexp = small[:, 4:6], small[:, 6:8]
    csil = small[:, 8:24]
    MOD = small[:, 24:120].rearrange("p (j e) -> p j e", e=2)
    G1, G1c, P1, G2, P2 = (small[:, 120 + 8 * i:128 + 8 * i] for i in range(5))
    dmx, dsum, drs, drl = (small[:, 160 + 8 * i:168 + 8 * i].rearrange("p (s e) -> p s e", e=2) for i in range(4))
    amx, anm, asum, ask, atot, arc = (small[:, 192 + 4 * i:196 + 4 * i] for i in range(6))

    PS = nc.alloc_psum_tensor("PS", [128, 8, T], f32).ap()

    def sem(name):
        return nc.alloc_semaphore(name)

    DVE, SCA, PE, POOL, SP = (Engine(sem(n)) for n in ("s_dve", "s_act", "s_pe", "s_pool", "s_sp"))

    def load(queue, name, dst, src, *after):
        s = sem(name)
        queue.dma(lambda: (nc.sync if queue is SP else nc.scalar).dma_start(dst, src), s, *after)
        return Token(s, 16)

    act_set = [None]

    def act(out_, in_, func, *after, bias=0.0, scale=1.0, accum=None):
        if func in (ACT.Exp, ACT.Ln):
            if act_set[0] != LN_EXP_SET:
                act_set[0] = LN_EXP_SET
                SCA.op(lambda: S.add_instruction(mybir.InstLoadActFuncSet(
                    name=nc.get_next_instruction_name(), act_func_set_id=LN_EXP_SET)), tick=False)
        elif func not in (ACT.Copy, ACT.Identity, ACT.Square):
            act_set[0] = func
        kw = {"accum_out": accum} if accum is not None else {}
        return SCA.op(lambda: S.activation(out_, in_, func, bias=bias, scale=scale, **kw), *after)

    def tt(out_, a_, b_, op, *after):
        return DVE.op(lambda: V.tensor_tensor(out_, a_, b_, op), *after)

    def ts(out_, a_, s1, s2, op0, op1, *after):
        return DVE.op(lambda: V.tensor_scalar(out_, a_, s1, s2, op0, op1), *after)

    def stt(out_, a_, s1, b_, op0, op1, *after):
        return DVE.op(lambda: V.scalar_tensor_tensor(out_, a_, s1, b_, op0, op1), *after)

    def mm(out_, l_, r_, start, stop, *after, tick=False, skip=False):
        return PE.op(lambda: E.matmul(out_, l_, r_, start=start, stop=stop, skip_group_check=skip), *after, tick=tick)

    t_vec = load(SP, "l_vec", vec, a["vec"])
    t_ones = load(SP, "l_ones", ones, a["consts"][:, CCOL["ones"][0]:CCOL["ones"][1]])
    t_x = [load(SP, f"l_x{i}", X[:, 2 * i:2 * i + 2, :], a["x"][:, 2 * i:2 * i + 2, :]) for i in range(4)]

    stream = []

    def chunks(name, kind="split", which=None):
        src = a[name]
        for i in (range(src.shape[0]) if which is None else which):
            stream.append((kind, src[i]))

    chunks("w_sq"), chunks("w_sk"), chunks("w_sv"), chunks("w_dv"), chunks("w_dq"), chunks("w_dk")
    chunks("w_mod", "raw")
    chunks("w_o"), chunks("w_up"), chunks("w_down")
    chunks("w_kv2"), chunks("w_q2"), chunks("w_f2"), chunks("w_g2"), chunks("w_dft")
    for i in range(4):
        chunks("w_pa", which=[i])
        chunks("w_pf", which=[i])
    chunks("w_out2"), chunks("w_up2"), chunks("w_down2")

    NR, NH, AHEAD = 5, 5, 3
    s_raw = [sem(f"s_raw{i}") for i in range(NR)]
    raw_done = {}
    hl_free = [None] * NH
    state = {"load": 0, "split": 0, "take": 0, "hl": 0}
    ready = {}

    def emit_loads():
        while state["load"] < len(stream):
            i = state["load"]
            if i >= NR and i - NR not in raw_done:
                return
            state["load"] += 1
            SP.dma(lambda i=i: nc.sync.dma_start(raw[i % NR], stream[i][1]), s_raw[i % NR], raw_done.get(i - NR))

    def landed(i):
        return Token(s_raw[i % NR], 16 * (i // NR + 1))

    def pump():
        while state["split"] < min(len(stream), state["take"] + AHEAD):
            i = state["split"]
            if i >= state["load"]:
                break
            if stream[i][0] == "raw":
                ready[i] = (raw[i % NR], None, landed(i), None)
                state["split"] += 1
                continue
            h = state["hl"] % NH
            if hl_free[h] == "busy":
                break
            r, hi, lo = raw[i % NR], whi[h], wlo[h]
            t_hi = act(hi, r, ACT.Copy, landed(i), hl_free[h])
            t_lo = tt(lo, r, hi.bitcast(f32), ALU.subtract, landed(i), hl_free[h], t_hi)
            hl_free[h] = "busy"
            ready[i] = (hi, lo, [t_hi, t_lo], h)
            raw_done[i] = [t_hi, t_lo, landed(i)]
            state["split"] += 1
            state["hl"] += 1
            emit_loads()

    def take():
        i = state["take"]
        state["take"] += 1
        pump()
        assert i in ready, i
        hi, lo, tok, h = ready[i]
        return {"i": i, "hi": hi, "lo": lo, "ready": tok, "h": h}

    def release(c, tok):
        if c["h"] is None:
            raw_done[c["i"]] = [tok, landed(c["i"])]
            emit_loads()
        else:
            hl_free[c["h"]] = tok
        pump()

    emit_loads()

    def const(name, dst, *after):
        lo, hi = CCOL[name]
        return load(SP, "l_" + name, dst, a["consts"][:, lo:hi], *after)

    t_ident, t_tri, t_blk, t_sbmask = (const(n, d) for n, d in (
        ("ident", ident), ("tri", tri), ("blk", blk), ("sbmask", sbmask)))
    t_eps = DVE.op(lambda: V.memset(epsc, EPS))
    t_one = DVE.op(lambda: V.memset(onec, 1.0))

    bank_free = [None] * 8

    def rstd(dst, bank, width, t_stat, dim, *after):
        t = act(dst, PS[:, bank, 0:width], ACT.Ln, t_stat, t_eps, *after, bias=epsc, scale=1.0 / dim)
        bank_free[bank] = t
        return act(dst, dst, ACT.Exp, t, scale=-0.5)

    def cut(hi, lo, v, *after):
        t_hi = act(hi, v, ACT.Copy, *after)
        t_lo = tt(lo, v, hi.bitcast(f32), ALU.subtract, t_hi, *after)
        return [t_hi, t_lo]

    def products(out_, lhs, rhs, first, last, ready_, tick=False):
        mm(out_, lhs[0], rhs[0], first, False, ready_)
        mm(out_, lhs[0], rhs[1], False, False)
        return mm(out_, lhs[1], rhs[0], False, last, tick=tick)

    def wtile(c, k):
        return c["hi"][:, 128 * k:128 * k + 128], c["lo"][:, 128 * k:128 * k + 128]

    def gemm_chunk(c, x, xready, bank, nk=8, off=0, width=T, last_use=True):
        for k in range(nk):
            t = products(PS[:, bank, 0:width], wtile(c, off + k), x(k), k == 0, k == nk - 1,
                         [xready(k), c["ready"], bank_free[bank] if k == 0 else None], tick=k == nk - 1)
        if last_use:
            release(c, t)
        return t

    def gemm_group(x, xready, banks, width=T):
        cs = [take() for _ in banks]
        toks = [None] * len(banks)
        for k in range(8):
            for j, (c, b) in enumerate(zip(cs, banks)):
                toks[j] = products(PS[:, b, 0:width], wtile(c, k), x(k), k == 0, k == 7,
                                   [xready(k), c["ready"], bank_free[b] if k == 0 else None], tick=k == 7)
        for c, t in zip(cs, toks):
            release(c, t)
        return toks

    def hx(k):
        return Hhi[:, k, :], Hlo[:, k, :]

    G_a = at("G_a", "G", 0, [128, T])
    G_b = at("G_b", "G", 2048, [128, T])
    G_c = at("G_c", "G", 4096, [128, T])
    G_d = at("G_d", "G", 6144, [128, T])
    G_r = at("G_r", "G", 8192, [128, T])
    G_s = at("G_s", "G", 10240, [128, T])

    def normed(src_ready, g, shift, stats_ready, h_free, src=X, width=T, hi=Hhi, lo=Hlo, bank=7, tmp=(G_a, G_b)):
        if stats_ready is None:
            free = [None, None]
            for c in range(8):
                sq = tmp[c % 2][:, 0:width]
                t = act(sq, src[:, c, 0:width], ACT.Square, src_ready[c], free[c % 2])
                stats_ready = free[c % 2] = mm(PS[:, bank, 0:width], ones, sq, c == 0, c == 7, t, t_ones,
                                               bank_free[bank] if c == 0 else None, tick=True)
            t_tmp = free
        else:
            t_tmp = [None, None]
        r = G_r[:, 0:width]
        t_r = rstd(r, bank, width, stats_ready, D)
        toks = []
        for c in range(8):
            v = tmp[c % 2][:, 0:width]
            t = tt(v, src[:, c, 0:width], r, ALU.mult, t_r, t_tmp[c % 2], src_ready[c])
            if shift is None:
                t = ts(v, v, g[:, c:c + 1], 1.0, ALU.mult, ALU.mult, t)
            else:
                t = ts(v, v, g[:, c:c + 1], shift(c), ALU.mult, ALU.add, t)
            t_tmp[c % 2] = cut(hi[:, c, 0:width], lo[:, c, 0:width], v, t, h_free)
            toks.append(t_tmp[c % 2])
        return toks, [t_r] + t_tmp

    t_xs = [t_x[c // 2] for c in range(8)]
    t_h, t_gfree = normed(t_xs, vc("g_pre1", n=8), None, None, t_vec)

    t = act(csil, vc("c", n=16), ACT.Silu, t_vec)
    t_csil = t
    t = DVE.op(lambda: V.tensor_tensor(lprod, vc("lam", n=2), vc("lam", 2, n=2), ALU.mult), t_vec)
    t = mm(PS[:, 6, 0:2], ones, lprod, True, True, t, t_ones, bank_free[6], tick=True)
    t = act(lexp, PS[:, 6, 0:2], ACT.Exp, t)
    bank_free[6] = t
    t = tt(lamc, lexp[:, 0:1], lexp[:, 1:2], ALU.subtract, t)
    t_lam = ts(lamc, lamc, LAM_INIT, 1.0, ALU.add, ALU.mult, t)
    t_gd = ts(gd, vc("subln"), 1.0 - LAM_INIT, 1.0, ALU.mult, ALU.mult, t_vec)

    onehot = at("onehot", "M", 0, [33, 640])
    tbl = at("tbl", "M", 2560, [33, 4, 128])
    brow = at("brow", "M", 4608, [128, 4, 640])
    t_oh = load(SP, "l_oh", onehot, a["onehot"])
    t_brow = []
    for h in range(4):
        t = ts(tbl[:, h, :], ones[0:33, :], vec[0:33, COL["table"][0] + h:COL["table"][0] + h + 1], 1.0, ALU.mult,
               ALU.mult, t_vec, t_ones)
        mm(PS[:, 5, 0:512], tbl[:, h, :], onehot[:, 0:512], True, True, t, t_oh, bank_free[5])
        t = mm(PS[:, 6, 0:128], tbl[:, h, :], onehot[:, 512:640], True, True, bank_free[6], tick=True)
        t1 = act(brow[:, h, 0:512], PS[:, 5, 0:512], ACT.Copy, t)
        t2 = act(brow[:, h, 512:640], PS[:, 6, 0:128], ACT.Copy, t)
        bank_free[5] = bank_free[6] = t2
        t_brow.append(t2)
    t_brow = load(SP, "l_brow", a["scratch"], brow, t_brow)

    QS, KS, QD, KD = (at(n, "A", 8192 * i, [128, 4, T]) for i, n in enumerate(("QS", "KS", "QD", "KD")))
    VS = at("VS", "A", 32768, [128, 4, T])
    VD = at("VD", "A", 40960, [128, 4, T])

    def evac(dst, src, bank, *after):
        t = act(dst, src, ACT.Copy, *after)
        bank_free[bank] = t
        return t

    def hr(k):
        return t_h[k]

    toks = gemm_group(hx, hr, [0, 1, 2, 3])
    t_qs = [evac(QS[:, j, :], PS[:, j, :], j, toks[j]) for j in range(4)]
    t_ks = []
    for j in range(4):
        b = 4 + j % 2
        t = gemm_chunk(take(), hx, hr, b)
        t_ks.append(evac(KS[:, j, :], PS[:, b, :], b, t))

    def gemm_v(dst, banks):
        for kc in range(4):
            c = take()
            for j in range(2):
                k = 2 * kc + j
                w = (c["hi"][:, 512 * j:512 * j + 512], c["lo"][:, 512 * j:512 * j + 512])
                for tq in range(4):
                    x = (Hhi[:, k, 128 * tq:128 * tq + 128], Hlo[:, k, 128 * tq:128 * tq + 128])
                    t = products(PS[:, banks[tq], :], x, w, k == 0, k == 7,
                                 [c["ready"], bank_free[banks[tq]] if k == 0 else None], tick=(k == 7 or tq == 3))
                    if k == 7:
                        yield_t[tq] = t
            release(c, t)
        return [evac(dst[:, tq, :], PS[:, banks[tq], :], banks[tq], yield_t[tq]) for tq in range(4)]

    yield_t = [None] * 4
    t_vs = gemm_v(VS, [0, 1, 2, 3])
    t_vd = gemm_v(VD, [4, 5, 6, 7])

    Mhi = at("Mhi", "M", 0, [128, 8, T], f32r)
    Mlo = at("Mlo", "M", 16384, [128, 8, T], f32r)
    Z = [at(f"Z{i}", "G", 4096 * i, [128, 2, T]) for i in range(3)]
    L0 = at("L0", "X", 0, [128, 2, 512])
    L1 = at("L1", "X", 4096, [128, 2, 384])
    L2 = at("L2", "X", 7168, [128, 2, 256])
    L3 = [at(f"L3{i}", "X", 9216 + 1024 * i, [128, 2, 128]) for i in range(2)]
    sbr = at("sbr", "X", 11264, [128, T])
    sbt = at("sbt", "X", 13312, [128, T])
    z_free = [t_gfree] * 3
    l_free = {k: t_h for k in ("L0", "L1", "L2", "L30", "L31")}
    x_scratch_done = []
    sbn_free = [t_h, t_h]
    t_mix = [None] * 8
    mix_free = [t_brow]

    def lbuf(j, kb):
        return [L0, L1, L2, L3[j % 2]][kb], ["L0", "L1", "L2", f"L3{j % 2}"][kb]

    def head_norm(bank_o, t_o, sbank, weight, dim, gcol, hi, lo, r, v, free, *after):
        t = act(r, PS[:, bank_o, :], ACT.Square, t_o, free[0])
        t = mm(PS[:, sbank, :], weight, r, True, True, t, bank_free[sbank], t_blk, tick=True)
        t_r = rstd(r, sbank, T, t, dim, t)
        t = tt(v, PS[:, bank_o, :], r, ALU.mult, t_r, free[1])
        bank_free[bank_o] = t
        free[0] = t
        t = ts(v, v, gcol, 1.0, ALU.mult, ALU.mult, t)
        tk = cut(hi, lo, v, t, *after)
        free[1] = tk
        return tk

    sb = {}

    def sb1(s):
        j, kb = s // 4, 3 - s % 4
        w = T - 128 * kb
        z = Z[s % 3]
        for e in range(2):
            p = slice(64 * e, 64 * e + 64)
            t = mm(PS[:, e, 0:w], KS[p, j, 128 * kb:128 * kb + 128], QS[p, j, 128 * kb:T], True, True,
                   bank_free[e], t_ks[j], t_qs[j], tick=True)
        t = stt(z[:, :, 0:w], PS[:, 0:2, 0:w], ZCAP, sbmask[:, None, 0:w].to_broadcast([128, 2, w]), ALU.min, ALU.add,
                t, t_sbmask, z_free[s % 3])
        bank_free[0] = bank_free[1] = t
        lb, name = lbuf(j, kb)
        t_e = act(lb, z[:, :, 0:w], ACT.Exp, t, l_free[name], scale=0.125)
        t_l = act(lb, lb, ACT.Ln, t_e, t_one, bias=onec)
        sb[s] = [t, t_e, t_l]

    def sb2(s):
        j, kb = s // 4, 3 - s % 4
        w = T - 128 * kb
        z = Z[s % 3]
        for e in range(2):
            t = mm(PS[:, 2 + e, 0:w], tri, lbuf(j, kb)[0][:, e, :], True, kb == 3, sb[s][2], bank_free[2 + e], t_tri,
                   tick=True)
            for jb in range(kb + 1, 4):
                o = 128 * (jb - kb)
                t = mm(PS[:, 2 + e, o:w], ones, lbuf(j, jb)[0][:, e, :], False, jb == 3, t_ones, tick=True)
        if kb == 0:
            for n in range(4):
                l_free[lbuf(j, n)[1]] = t
        t_a = stt(z[:, :, 0:w], z[:, :, 0:w], 0.125, PS[:, 2:4, 0:w], ALU.mult, ALU.subtract, t, sb[s][1])
        bank_free[2] = bank_free[3] = t_a
        sb[s] = act(z[:, :, 0:w], z[:, :, 0:w], ACT.Exp, t_a)

    def sb3(s):
        j, kb = s // 4, 3 - s % 4
        w = T - 128 * kb
        z = Z[s % 3]
        for e in range(2):
            t = mm(PS[64 * e:64 * e + 64, 4, 128 * kb:T], VS[:, kb, 128 * j + 64 * e:128 * j + 64 * e + 64],
                   z[:, e, 0:w], kb == 3, kb == 0, sb[s], t_vs[kb], bank_free[4] if kb == 3 else None,
                   tick=True, skip=True)
        z_free[s % 3] = t
        if kb == 0:
            t_mix[4 + j] = head_norm(4, t, 5, blk, 64, vc("sbn"), Mhi[:, 4 + j, :], Mlo[:, 4 + j, :], sbr, sbt,
                                     sbn_free, mix_free[0])
            x_scratch_done[:] = [t_mix[4 + j], sbn_free[0]]

    t_qd, t_kd = [], []

    def qk_diff(n):
        c = take()
        b = 6 + n % 2
        t = gemm_chunk(c, hx, hr, b)
        if n < 4:
            t_qd.append(evac(QD[:, n, :], PS[:, b, :], b, t))
        else:
            t_kd.append(evac(KD[:, n - 4, :], PS[:, b, :], b, t))

    for tick in range(18):
        if tick < 16:
            sb1(tick)
        if 1 <= tick < 17:
            sb2(tick - 1)
        if tick % 2 == 0 and tick < 16:
            qk_diff(tick // 2)
        if tick >= 2:
            sb3(tick - 2)
    t_hfree = Token(PE.sem, PE.n)

    BW = at("BW", "H", 0, [128, 4, 512])
    DL = [at(f"DL{i}", "H", 8192 + 4096 * i, [128, 2, 512]) for i in range(3)]
    DW = [at(f"DW{i}", "H", 20480 + 2048 * i, [128, 512]) for i in range(2)]
    DT = [at(f"DT{i}", "H", 24576 + 2048 * i, [128, 512]) for i in range(2)]
    dnr = at("dnr", "H", 28672, [128, T])
    dnv = at("dnv", "H", 30720, [128, T])
    win = bass.AP(tensor=a["scratch"].tensor, offset=127, ap=[[4 * 640 - 1, 128], [640, 4], [1, 512]])
    t_bw = load(SP, "l_bw", BW, win, t_brow, t_hfree)
    dl_free, dw_free, dt_free, dn_free = [t_hfree] * 3, [t_hfree] * 2, [t_hfree] * 2, [t_hfree, t_hfree]
    df = {}

    def d1(s):
        h, qb = s // 4, s % 4
        n = 128 * (qb + 1)
        l, b = DL[s % 3], 2 * (s % 2)
        for e in range(2):
            p = slice(64 * e, 64 * e + 64)
            t = mm(PS[:, b + e, 0:n], QD[p, h, 128 * qb:128 * qb + 128], KD[p, h, 0:n], True, True, bank_free[b + e],
                   t_qd[h], t_kd[h], tick=True)
        t = stt(l[:, :, 0:n], PS[:, b:b + 2, 0:n], 0.125, BW[:, h:h + 1, 512 - n:512].to_broadcast([128, 2, n]),
                ALU.mult, ALU.add, t, t_bw, dl_free[s % 3])
        bank_free[b] = bank_free[b + 1] = t
        m, sm = dmx[:, s % 4, :], dsum[:, s % 4, :]
        t_m = DVE.op(lambda: V.tensor_reduce(m, l[:, :, 0:n], AX.X, ALU.max, negate=True), t)
        for e in range(2):
            t_e = act(l[:, e, 0:n], l[:, e, 0:n], ACT.Exp, t_m, bias=m[:, e:e + 1], accum=sm[:, e:e + 1])
        df[s] = t_e

    def d2(s):
        n = 128 * (s % 4 + 1)
        l, w, q = DL[s % 3], DW[s % 2], s % 4
        t = DVE.op(lambda: V.reciprocal(drs[:, q, :], dsum[:, q, :]), df[s])
        t = tt(drl[:, q, 0:1], drs[:, q, 1:2], lamc, ALU.mult, t, t_lam)
        t = ts(w[:, 0:n], l[:, 1, 0:n], drl[:, q, 0:1], 1.0, ALU.mult, ALU.mult, t, dw_free[s % 2])
        t = stt(w[:, 0:n], l[:, 0, 0:n], drs[:, q, 0:1], w[:, 0:n], ALU.mult, ALU.subtract, t)
        dl_free[s % 3] = df[s] = t

    def d3(s):
        nb = s % 4 + 1
        w, wt = DW[s % 2], DT[s % 2]
        for i in range(nb):
            t = PE.op(lambda i=i: E.transpose(PS[:, 4, 128 * i:128 * i + 128], w[:, 128 * i:128 * i + 128], ident),
                      df[s], t_ident, bank_free[4])
        dw_free[s % 2] = t
        t = evac(wt[:, 0:128 * nb], PS[:, 4, 0:128 * nb], 4, t, dt_free[s % 2])
        df[s] = t

    def d4(s):
        h, qb = s // 4, s % 4
        wt = DT[s % 2]
        for i in range(qb + 1):
            t = mm(PS[:, 5, 128 * qb:128 * qb + 128], VD[:, i, 128 * h:128 * h + 128], wt[:, 128 * i:128 * i + 128],
                   i == 0, i == qb, df[s], t_vd[i], bank_free[5] if qb == 0 else None, tick=True)
        dt_free[s % 2] = t
        if qb == 3:
            t_mix[h] = head_norm(5, t, 7, ones, 128, gd, Mhi[:, h, :], Mlo[:, h, :], dnr, dnv, dn_free, t_gd, mix_free[0])

    mod_tok = [None]

    def mod_chunk():
        c = take()
        j = c["i"] - 24
        for k in range(8):
            mod_tok[0] = mm(PS[:, 6, 2 * j:2 * j + 2], c["hi"][:, 128 * k:128 * k + 128], csil[:, 2 * k:2 * k + 2],
                            k == 0, k == 7, c["ready"], t_csil, bank_free[6] if j == 0 and k == 0 else None, tick=k == 7)
        release(c, mod_tok[0])

    n_mod = 0
    assert state["take"] == 24
    for tick in range(19):
        if tick < 16:
            d1(tick)
        if n_mod < 48:
            mod_chunk()
            n_mod += 1
        if 1 <= tick < 17:
            d2(tick - 1)
        if 2 <= tick < 18:
            d3(tick - 2)
        for _ in range(2):
            if n_mod < 48:
                mod_chunk()
                n_mod += 1
        if tick >= 3:
            d4(tick - 3)
    t_xback = load(SP, "l_xback", X, a["x"], x_scratch_done)
    t_atfree = Token(PE.sem, PE.n)

    t = tt(MOD, PS[:, 6, 0:96].rearrange("p (j e) -> p j e", e=2),
           vc("bmod", n=48).unsqueeze(2).to_broadcast([128, 48, 2]), ALU.add, mod_tok[0])
    bank_free[6] = t
    t = stt(G1, MOD[:, 8:16, 0], 1.0, vc("h_pre1", n=8), ALU.add, ALU.mult, t)
    stt(G1c, MOD[:, 8:16, 1], 1.0, vc("h_pre1", n=8), ALU.add, ALU.mult)
    tt(P1, MOD[:, 16:24, 0], vc("h_post1", n=8), ALU.mult)
    stt(G2, MOD[:, 32:40, 0], 1.0, vc("h_pre2", n=8), ALU.add, ALU.mult)
    t_mod = tt(P2, MOD[:, 40:48, 0], vc("h_post2", n=8), ALU.mult)

    Y_A = at("Y_A", "A", 0, [128, 8, T])
    Y_M = at("Y_M", "M", 0, [128, 8, T])

    class Post:

        def __init__(self, y, y_free, *after):
            self.y, self.y_free, self.after = y, y_free, after
            self.t_y, self.t_acc, self.sqf = [], None, [None, None]

        def chunk(self, c, bank, t):
            t_y = act(self.y[:, c, :], PS[:, bank, :], ACT.Copy, t, self.y_free)
            sq = G_s if c == 0 else (G_a, G_b)[c % 2]
            t_q = act(sq, PS[:, bank, :], ACT.Square, t, self.sqf[c % 2], self.after)
            bank_free[bank] = t_q
            if c == 0:
                self.t_acc = t_q
            else:
                self.t_acc = self.sqf[c % 2] = tt(G_s, G_s, sq, ALU.add, t_q, self.t_acc)
            self.t_y.append(t_y)

        def finish(self, g, x_ready, bank, pre, out_dram=None):
            t = mm(PS[:, bank, :], ones, G_s, True, True, self.t_acc, bank_free[bank], tick=True)
            t_r = rstd(G_r, bank, T, t, D)
            toks, stat, free = [], None, [self.sqf, self.sqf]
            for c in range(8):
                v = (G_a, G_b)[c % 2]
                t = tt(v, self.y[:, c, :], G_r, ALU.mult, t_r, self.t_y[c], free[c % 2])
                t = free[c % 2] = stt(X[:, c, :], v, g[:, c:c + 1], X[:, c, :], ALU.mult, ALU.add, t, x_ready)
                toks.append(t)
                if pre:
                    sq = (G_c, G_d)[c % 2]
                    t = act(sq, X[:, c, :], ACT.Square, t, sqm[c % 2])
                    stat = sqm[c % 2] = mm(PS[:, bank2, :], ones, sq, c == 0, c == 7, t,
                                           bank_free[bank2] if c == 0 else None, tick=True)
                if out_dram is not None:
                    o = sem(f"s_out{c}")
                    SP.dma(lambda c=c: nc.sync.dma_start(out_dram[:, c, :], X[:, c, :]), o, t)
                    outs.append(Token(o, 16))
            return toks, stat, [toks, t_r]

    outs = []
    sqm = [None, None]
    bank2 = 6

    post = Post(Y_A, t_atfree, z_free)
    for o in range(8):
        b = o % 5

        def mixt(k):
            k = (4, 5, 6, 7, 0, 1, 2, 3)[k]
            return Mhi[:, k, :], Mlo[:, k, :]

        c = take()
        for i, k in enumerate((4, 5, 6, 7, 0, 1, 2, 3)):
            t = products(PS[:, b, :], wtile(c, k), (Mhi[:, k, :], Mlo[:, k, :]), i == 0, i == 7,
                         [t_mix[k], c["ready"], bank_free[b] if i == 0 else None], tick=i == 7)
        release(c, t)
        post.chunk(o, b, t)
    t_mixfree = t
    t_x1, t_stat, fr = post.finish(vc("g_post1", n=8), [t_xback, t_vec], 7, True)
    t_h, t_gf = normed(t_x1, vc("g_pre2", n=8), None, t_stat, [dn_free, t_mixfree, fr], bank=bank2)

    ACTV = at("ACTV", "A", 0, [128, NF, T])
    C = [at(f"C{i}", "M", 2048 * i, [128, T]) for i in range(8)]
    y_free = t_x1
    c_free = [t_mixfree] * 8

    def conv(bank, t, buf, taps, bias, shifts, i):
        dst = C[buf]
        mid = shifts.index(0)
        t = act(dst, PS[:, bank, :], ACT.Identity, t, c_free[buf], bias=bias, scale=taps[mid])
        for tap, sh in zip(taps, shifts):
            if sh == 0:
                continue
            if sh < 0:
                o_, i_ = dst[:, -sh:T], PS[:, bank, 0:T + sh]
            else:
                o_, i_ = dst[:, 0:T - sh], PS[:, bank, sh:T]
            t = stt(o_, i_, tap, o_, ALU.mult, ALU.add, t)
        bank_free[bank] = t
        return t

    act_ready = [None] * NF

    def up1(n, bank, t):
        f, is_val = n // 2, n % 2
        col = f + NF * is_val
        t = conv(bank, t, n % 4, [vc("cw", 44 * i + col) for i in range(3)], vc("cb", col), [-2, -1, 0], col)
        if not is_val:
            held[0] = act(C[n % 4], C[n % 4], ACT.Gelu_apprx_tanh, t)
        else:
            t = tt(ACTV[:, f, :], C[(n - 1) % 4], C[n % 4], ALU.mult, t, held[0], y_free)
            c_free[(n - 1) % 4] = c_free[n % 4] = t
            act_ready[f] = t

    held = [None]

    def up_phase(handler):
        toks = gemm_group(hx, lambda k: t_h[k], [0, 1, 2, 3])
        for n in range(4):
            handler(n, n, toks[n])
        for n in range(4, 2 * NF):
            b = 4 + n % 4 if n < 8 else n % 6
            handler(n, b, gemm_chunk(take(), hx, lambda k: t_h[k], b))

    up_phase(up1)
    t_upfree = Token(PE.sem, PE.n)

    Dhi = [at(f"Dhi{i}", "H", 4096 * i, [128, T], f32r) for i in range(8)]
    Dlo = [at(f"Dlo{i}", "H", 4096 * i + 2048, [128, T], f32r) for i in range(8)]

    def down_phase(post):
        d_free = [t_upfree] * 8
        d_tok = {}

        def prep(f):
            d_tok[f] = cut(Dhi[f % 8], Dlo[f % 8], ACTV[:, f, :], act_ready[f], d_free[f % 8])

        for f in range(3):
            prep(f)
        tail = 4
        for f in range(NF - tail):
            if f + 3 < NF:
                prep(f + 3)
            c = take()
            for o in range(8):
                t = products(PS[:, o, :], wtile(c, o), (Dhi[f % 8], Dlo[f % 8]), f == 0, False,
                             [d_tok[f], c["ready"], bank_free[o] if f == 0 else None], tick=o == 7)
            release(c, t)
            d_free[f % 8] = t
        prep(NF - 1)
        cs = [take() for _ in range(tail)]
        for o in range(8):
            for i, c in enumerate(cs):
                f = NF - tail + i
                t = products(PS[:, o, :], wtile(c, o), (Dhi[f % 8], Dlo[f % 8]), False, i == tail - 1,
                             [d_tok[f], c["ready"]], tick=i == tail - 1)
            post.chunk(o, o, t)
        for c in cs:
            release(c, t)
        return t

    post = Post(Y_M, c_free, t_gf)
    t_down = down_phase(post)
    t_x2, t_stat, fr = post.finish(vc("g_post2", n=8), [t_x1], 0, True)
    t_h, t_gf = normed(t_x2, G1, lambda c: MOD[:, c, 0:1], t_stat, [t_down, t_mod, fr], bank=bank2)

    Xc = at("Xc", "M", 0, [128, 8, 256])
    HChi = at("HChi", "M", 8192, [128, 8, 256], f32r)
    HClo = at("HClo", "M", 16384, [128, 8, 256], f32r)
    Mc_a = at("Mc_a", "M", 24576, [128, 256])
    Mc_b = at("Mc_b", "M", 25600, [128, 256])
    t_xc = load(SP, "l_xc", Xc, a["ctx"], t_x2)
    t_hc, t_gf2 = normed([t_xc] * 8, G1c, lambda c: MOD[:, c, 1:2], None, [t_x2, t_mod, t_gf], src=Xc, width=256,
                         hi=HChi, lo=HClo, bank=7, tmp=(Mc_a, Mc_b))

    Q2 = at("Q2", "A", 0, [128, 4, T])
    K2 = at("K2", "A", 8192, [128, T])
    V2 = at("V2", "A", 10240, [128, 4, 128])
    KC = at("KC", "A", 12288, [128, 256])
    VC = at("VC", "A", 13312, [128, 2, 128])
    Fhi = at("Fhi", "A", 14336, [128, 4, T], f32r)
    Flo = at("Flo", "A", 22528, [128, 4, T], f32r)
    AThi = at("AThi", "A", 30720, [128, 4, T], f32r)
    ATlo = at("ATlo", "A", 38912, [128, 4, T], f32r)
    ropeC = at("ropeC", "G", 8192, [128, T])
    ropeS = at("ropeS", "G", 10240, [128, T])
    a_free = t_down
    hr2 = lambda k: t_h[k]

    c = take()
    t = gemm_chunk(c, hx, hr2, 0, last_use=False)
    t_k2 = evac(K2, PS[:, 0, :], 0, t, a_free, post.t_acc)
    t = gemm_chunk(c, lambda k: (HChi[:, k, :], HClo[:, k, :]), lambda k: t_hc[k], 1, width=256)
    t_kc = evac(KC, PS[:, 1, 0:256], 1, t, a_free)
    c = take()
    for tq in range(6):
        for k in range(8):
            if tq < 4:
                x = (Hhi[:, k, 128 * tq:128 * tq + 128], Hlo[:, k, 128 * tq:128 * tq + 128])
            else:
                x = (HChi[:, k, 128 * tq - 512:128 * tq - 384], HClo[:, k, 128 * tq - 512:128 * tq - 384])
            b = 2 + tq % 2
            t = products(PS[:, b, 0:128], x, wtile(c, k), k == 0, k == 7,
                         [c["ready"], t_h[k], t_hc[k] if tq >= 4 else None, bank_free[b] if k == 0 else None], tick=k == 7)
        t_v2 = evac(V2[:, tq, :] if tq < 4 else VC[:, tq - 4, :], PS[:, b, 0:128], b, t, a_free)
    release(c, t)
    t_hcfree = t

    permc = at("permc", "M", 28672, [128, 128])
    t_perm = load(SP, "l_perm", permc, a["consts"][:, CCOL["perm"][0]:CCOL["perm"][1]], [t_x2, c_free])
    t_rc = load(SP, "l_rc", ropeC, a["rope"][:, 0, :], [t_h, t_gf2])
    t_rs = load(SP, "l_rs", ropeS, a["rope"][:, 1, :], [t_h, t_gf2])
    rt = [t_gf2]

    def rope(x, t_x):
        t = mm(PS[:, 5, :], permc, x, True, True, t_x, t_perm, bank_free[5], tick=True)
        t2 = tt(G_b, PS[:, 5, :], ropeS, ALU.mult, t, t_rs, rt[0])
        bank_free[5] = t2
        t3 = tt(x, x, ropeC, ALU.mult, t, t_rc)
        rt[0] = tt(x, x, G_b, ALU.add, t2, t3)
        return rt[0]

    t_k2 = rope(K2, t_k2)
    t_q2 = []
    for j in range(4):
        b = 3 + j % 2
        t = gemm_chunk(take(), hx, hr2, b)
        t = evac(Q2[:, j, :], PS[:, b, :], b, t)
        t_q2.append(rope(Q2[:, j, :], t))

    P2b = [at(f"P2b{i}", "G", 2560 * i, [128, 640]) for i in range(2)]
    PT2 = [at(f"PT2{i}", "G", 5120 + 2560 * i, [128, 640]) for i in range(2)]
    O2 = [at(f"O2{i}", "G", 10240 + 512 * i, [128, 128]) for i in range(4)]
    OT = [at(f"OT{i}", "A", 47104 + 512 * i, [128, 128]) for i in range(4)]
    GT = at("GT", "M", 0, [128, 16, T])
    bmf = at("bmf", "M", 29184, [128, 2, 128])
    t_bm = load(SP, "l_bm", bmf, a["consts"][:, CCOL["mlow"][0]:CCOL["mhigh"][1]].rearrange("p (a b) -> p a b", a=2),
                [t_x2, c_free])
    t1 = ts(mlowb, bmf[:, 0, :], 1.0, 1.0, ALU.mult, ALU.mult, t_bm)
    t2 = ts(mhighb, bmf[:, 1, :], 1.0, 1.0, ALU.mult, ALU.mult, t_bm)
    t3 = ts(identb, ident, 1.0, 1.0, ALU.mult, ALU.mult, t_ident)
    t_masks = [t1, t2, t3]
    g_all = [rt[0], t_k2, t_q2]
    p_free, pt_free, o2_free, ot_free = [g_all] * 2, [g_all] * 2, [g_all] * 4, [a_free] * 4
    at_tok = [[] for _ in range(4)]
    ab = {}

    def geom(s):
        j, qb, e = s // 8, s // 2 % 4, s % 2
        k0, k1 = max(qb - 1, 0), min(qb + 1, 3)
        return j, qb, e, k0, k1 - k0 + 1

    def a1(s):
        j, qb, e, k0, nl = geom(s)
        n, b = 128 * (nl + 2), 2 * (s % 2)
        p = slice(64 * e, 64 * e + 64)
        q = Q2[p, j, 128 * qb:128 * qb + 128]
        flat = PS[:, b:b + 2, :].rearrange("p a b -> p (a b)")
        masks = [(0, mlowb)] * (qb > 0) + [(128 * (nl - 1), mhighb)] * (qb < 3)
        mm(flat[:, 0:128 * nl], q, K2[p, 128 * k0:128 * (k0 + nl)], True, False, bank_free[b], bank_free[b + 1],
           t_q2[j], t_k2, t_kc)
        for i, (o, m) in enumerate(masks):
            t = mm(flat[:, o:o + 128], identb, m, False, i == len(masks) - 1, t_masks)
        if nl == 2:
            t = mm(flat[:, 256:512], q, KC[p, :], True, True, tick=True)
        else:
            mm(flat[:, 384:512], q, KC[p, 0:128], True, True)
            t = mm(flat[:, 512:640], q, KC[p, 128:256], True, True, tick=True)
        i = s % 4
        h = j + 4 * e
        m, sm = amx[:, i:i + 1], asum[:, i:i + 1]
        t_m = DVE.op(lambda: V.tensor_reduce(m, flat[:, 0:n], AX.X, ALU.max), t)
        t_m = ts(anm[:, i:i + 1], m, 0.125, vc("sink", h), ALU.mult, ALU.max, t_m)
        t_m = ts(anm[:, i:i + 1], anm[:, i:i + 1], -1.0, 1.0, ALU.mult, ALU.mult, t_m)
        t_e = act(P2b[s % 2][:, 0:n], flat[:, 0:n], ACT.Exp, t_m, p_free[s % 2], bias=anm[:, i:i + 1], scale=0.125,
                  accum=sm)
        bank_free[b] = bank_free[b + 1] = t_e
        t_s = act(ask[:, i:i + 1], vc("sink", h), ACT.Exp, t_m, bias=anm[:, i:i + 1])
        t = tt(atot[:, i:i + 1], sm, ask[:, i:i + 1], ALU.add, t_e, t_s)
        t = DVE.op(lambda: V.reciprocal(arc[:, i:i + 1], atot[:, i:i + 1]), t)
        ab[s] = [t_e, t]

    def a2(s):
        j, qb, e, k0, nl = geom(s)
        n = nl + 2
        t_e, t_r = ab[s]
        p, pt = P2b[s % 2], PT2[s % 2]
        tp = PS[:, 4:6, :].rearrange("p a b -> p (a b)")
        for i in range(n):
            t = PE.op(lambda i=i: E.transpose(tp[:, 128 * i:128 * i + 128], p[:, 128 * i:128 * i + 128], ident),
                      t_e, t_ident, bank_free[4], bank_free[5])
        p_free[s % 2] = t
        t = evac(pt[:, 0:128 * n], tp[:, 0:128 * n], 4, t, pt_free[s % 2])
        bank_free[5] = t
        ab[s] = [t, t_r]

    def a3(s):
        j, qb, e, k0, nl = geom(s)
        n = nl + 2
        t_pt, t_r = ab[s]
        pt = PT2[s % 2]
        o = PS[:, 6, 64 * (s % 2):64 * (s % 2) + 64]
        for i in range(n):
            v = V2[:, k0 + i, 64 * e:64 * e + 64] if i < nl else VC[:, i - nl, 64 * e:64 * e + 64]
            t = mm(o, pt[:, 128 * i:128 * i + 128], v, i == 0, i == n - 1, t_pt, t_v2, bank_free[6], tick=True)
        pt_free[s % 2] = t
        r = s // 2 % 4
        i = s % 4
        t = ts(O2[r][:, 64 * e:64 * e + 64], o, arc[:, i:i + 1], 1.0, ALU.mult, ALU.mult, t, t_r, o2_free[r])
        bank_free[6] = t
        ab[s] = t

    def a4(s):
        j, qb, e, k0, nl = geom(s)
        if not e:
            return
        r = s // 2 % 4
        q = slice(128 * qb, 128 * qb + 128)
        t = PE.op(lambda: E.transpose(PS[:, 6, 128:256], O2[r], ident), ab[s], ab[s - 1], bank_free[6])
        o2_free[r] = t
        t_o = act(OT[r], PS[:, 6, 128:256], ACT.Copy, t, ot_free[r])
        bank_free[6] = t_o
        ot_free[r] = cut(AThi[:, j, q], ATlo[:, j, q], OT[r], t_o, a_free)
        at_tok[j].append(ot_free[r])

    fills = [("f", i) for i in range(4)] + [("g", i) for i in range(16)]
    t_f, t_g = [], [None] * 16

    def fill():
        kind, i = fills.pop(0)
        t = gemm_chunk(take(), hx, hr2, 7)
        if kind == "f":
            t_hi = act(Fhi[:, i, :], PS[:, 7, :], ACT.Copy, t, a_free)
            t_lo = tt(Flo[:, i, :], PS[:, 7, :], Fhi[:, i, :].bitcast(f32), ALU.subtract, t_hi)
            bank_free[7] = t_lo
            t_f.append([t_hi, t_lo])
        else:
            t_g[i] = evac(GT[:, i, :], PS[:, 7, :], 7, t, t_hcfree, t_xc, rt[0], t_masks, t_hc)

    for tick in range(36):
        if tick < 32:
            a1(tick)
        if 3 <= tick < 35:
            a3(tick - 3)
        if fills and tick * 20 // 34 > 20 - len(fills) - 1:
            fill()
        if 1 <= tick < 33:
            a2(tick - 1)
        if tick >= 4:
            a4(tick - 4)
    while fills:
        fill()
    t_h2free = Token(PE.sem, PE.n)

    FT = at("FT", "A", 47104, [128, 256])
    ccs = at("ccs", "G", 0, [128, 256])
    cchi = at("cchi", "G", 1024, [128, 256], f32r)
    cclo = at("cclo", "G", 2048, [128, 256], f32r)
    ABhi = at("ABhi", "H", 0, [128, 4, 4, 256], f32r)
    AThi_all = [x for y in at_tok for x in y]
    t = load(SP, "l_ccs", ccs, a["consts"][:, CCOL["cc"][0]:CCOL["sc"][1]], [t_h2free, AThi_all])
    t_cc = cut(cchi, cclo, ccs, t)
    ABlo = at("ABlo", "H", 16384, [128, 4, 4, 256], f32r)
    t_ab = {}
    n = 0
    for g in range(4):
        for st in range(4):
            b = n % 4
            n += 1
            t = products(PS[:, b, 0:256], (Fhi[:, g, 128 * st:128 * st + 128], Flo[:, g, 128 * st:128 * st + 128]),
                         (cchi, cclo), True, True, [t_f[g], t_cc, bank_free[b]], tick=True)
            t_hi = act(ABhi[:, g, st, :], PS[:, b, 0:256], ACT.Copy, t, t_h2free)
            t_lo = tt(ABlo[:, g, st, :], PS[:, b, 0:256], ABhi[:, g, st, :].bitcast(f32), ALU.subtract, t_hi)
            bank_free[b] = t_lo
            t_ab[g, st] = [t_hi, t_lo]
    FOhi = at("FOhi", "A", 14336, [128, 4, T], f32r)
    FOlo = at("FOlo", "A", 22528, [128, 4, T], f32r)
    cs = [take() for _ in range(4)]
    t_fo, fo_free = [], t
    for g in range(4):
        b = 4 + g % 2
        i = 0
        for trig in range(2):
            for st in range(4):
                c = cs[2 * trig + st // 2]
                w = (c["hi"][:, 512 * (st % 2):512 * (st % 2) + 512], c["lo"][:, 512 * (st % 2):512 * (st % 2) + 512])
                x = (ABhi[:, g, st, 128 * trig:128 * trig + 128], ABlo[:, g, st, 128 * trig:128 * trig + 128])
                t = products(PS[:, b, :], x, w, i == 0, i == 7,
                             [t_ab[g, st], c["ready"], bank_free[b] if i == 0 else None], tick=i == 7)
                i += 1
        t_hi = act(FOhi[:, g, :], PS[:, b, :], ACT.Copy, t, fo_free)
        t_lo = tt(FOlo[:, g, :], PS[:, b, :], FOhi[:, g, :].bitcast(f32), ALU.subtract, t_hi)
        bank_free[b] = t_lo
        t_fo.append([t_hi, t_lo])
    for c in cs:
        release(c, t)
    t_abfree = t

    MGhi = at("MGhi", "H", 0, [128, 8, T], f32r)
    MGlo = at("MGlo", "H", 16384, [128, 8, T], f32r)
    mg_free = [None, None]
    t_sig = [None] * 16
    t_mg = []
    mt = [(at("mt0", "G", 3072, [128, T]), at("mt1", "G", 5120, [128, T])),
          (at("mt2", "G", 7168, [128, T]), at("mt3", "G", 9216, [128, T]))]
    mt_free = [[t_cc, AThi_all, ot_free], [t_cc, AThi_all, ot_free]]
    for o2 in range(4):
        ca, cf = take(), take()
        for e in range(2):
            o = 2 * o2 + e
            b = 2 * (o % 3)
            for i in (o, 8 + o):
                t_sig[i] = act(GT[:, i, :], GT[:, i, :], ACT.Sigmoid, t_g[i])
            t_a = gemm_chunk(ca, lambda k: (AThi[:, k, :], ATlo[:, k, :]), lambda k: at_tok[k], b, nk=4, off=4 * e,
                             last_use=e == 1)
            t_b = gemm_chunk(cf, lambda k: (FOhi[:, k, :], FOlo[:, k, :]), lambda k: t_fo[k], b + 1, nk=4, off=4 * e,
                             last_use=e == 1)
            u, v = mt[o % 2]
            ta = tt(u, PS[:, b, :], GT[:, o, :], ALU.mult, t_a, t_sig[o], mt_free[o % 2])
            tb = tt(v, PS[:, b + 1, :], GT[:, 8 + o, :], ALU.mult, t_b, t_sig[8 + o])
            bank_free[b], bank_free[b + 1] = ta, tb
            t = tt(u, u, v, ALU.add, ta, tb)
            mt_free[o % 2] = cut(MGhi[:, o, :], MGlo[:, o, :], u, t, t_abfree)
            t_mg.append(mt_free[o % 2])
    t_gtfree = [t_mg, ta, tb]

    post = Post(Y_M, t_gtfree, t_mg)
    for o in range(8):
        b = (0, 1, 2, 3, 4)[o % 5]
        t = gemm_chunk(take(), lambda k: (MGhi[:, k, :], MGlo[:, k, :]), lambda k: t_mg[k], b)
        post.chunk(o, b, t)
    t_mgfree = t
    t_x3, t_stat, fr = post.finish(P1, [t_x2, t_mod], 7, True)
    t_h, t_gf = normed(t_x3, G2, lambda c: MOD[:, 24 + c, 0:1], t_stat, [t_mgfree, fr], bank=bank2)

    y_free = [t_x3, t_mgfree, t_fo]
    c_free = [t_x3] * 8

    def up2(n, bank, t):
        f = n // 2
        if n % 2 == 0:
            t = conv(bank, t, f % 4, [vc("dw", NF * i + f) for i in range(3)], vc("db", f), [-1, 0, 1], f)
            held[0] = act(C[f % 4], C[f % 4], ACT.Silu, t)
        else:
            t = tt(ACTV[:, f, :], PS[:, bank, :], C[f % 4], ALU.mult, t, held[0], y_free)
            bank_free[bank] = t
            c_free[f % 4] = t
            act_ready[f] = t

    up_phase(up2)
    t_upfree = Token(PE.sem, PE.n)
    post = Post(Y_M, c_free, t_gf)
    down_phase(post)
    post.finish(P2, [t_x3], 0, False, out_dram=out)
    assert state["take"] == len(stream)
    s_end = sem("s_end")
    SP.queue.append((lambda: nc.sync.nop(), tuple(outs), (s_end, 1)))

    with nc.Block() as block:
        @block.sync
        def _(e):
            SP.run(e)

        @block.scalar
        def _(e):
            SCA.run(e)

        @block.vector
        def _(e):
            DVE.run(e)

        @block.tensor
        def _(e):
            PE.run(e)



def _shapes_only():
    i = np.arange(128)
    k, q = i[:, None], i[None, :]
    c = np.zeros((128, NC), np.float32)

    def put(name, v):
        c[:, CCOL[name][0]:CCOL[name][1]] = v

    put("ident", np.eye(128))
    put("ones", 1.0)
    put("tri", k >= q)
    put("blk", (k // 64) == (q // 64))
    m = np.zeros((128, 512))
    m[:, :128] = np.where(k < q, 0.0, SBNEG)
    put("sbmask", m)
    put("mlow", np.where(q >= k, 0.0, NEG))
    put("mhigh", np.where(q <= k, 0.0, NEG))
    d = i % 32
    src = np.where(d < 16, i + 16, i - 16)
    put("perm", (i[:, None] == src[None, :]))
    cc = np.outer(i, i) % 128 * (2 * np.pi / 128)
    norm = 1.0 / math.sqrt(512 * 128)
    put("cc", np.cos(cc))
    put("sc", -np.sin(cc))

    rel = 511 - np.arange(640)
    n = np.maximum(rel, 0)
    nf = np.maximum(n, 1).astype(np.float32)
    large = 16 + (np.log(nf / np.float32(16)) / np.float32(math.log(8)) * np.float32(16)).astype(np.int32)
    bucket = np.where(n < 16, n, np.minimum(large, 31))
    onehot = np.zeros((33, 640), np.float32)
    onehot[bucket, np.arange(640)] = 1.0
    onehot[:, rel < 0] = 0.0
    onehot[32, rel < 0] = 1.0

    t = np.arange(512)
    row, col = (t // 64).astype(np.float32), (t % 64).astype(np.float32)
    inv = (np.float32(10000.0) ** (-np.arange(0, 32, 2, dtype=np.float32) / np.float32(32))).astype(np.float32)
    rope = np.zeros((128, 2, 512), np.float32)
    for p in range(128):
        pos = row if p % 64 < 32 else col
        ang = (pos * inv[p % 16]).astype(np.float32)
        rope[p, 0] = np.cos(ang)
        rope[p, 1] = np.sin(ang) * (-1.0 if p % 32 < 16 else 1.0)

    ang = np.outer(t, t) % 512 * (2 * np.pi / 512)
    dft = np.stack([np.cos(ang) * norm, np.sin(ang) * norm]).astype(np.float32)
    dft = dft.reshape(2, 2, 2, 128, 512).transpose(0, 1, 3, 2, 4).reshape(4, 128, 1024)
    return c, onehot, rope, np.ascontiguousarray(dft)


def kernel(**inputs):
    import concourse.bacc as _bacc
    from concourse.bass_utils import run_bass_kernel_spmd as _run

    x = {k: np.asarray(v) for k, v in inputs.items()}
    f = np.float32

    def cols(v):
        return np.ascontiguousarray(v).reshape(-1, 128).T

    def by_out(w):
        k, n = w.shape
        return np.ascontiguousarray(
            w.reshape(k // 128, 128, n // 128, 128).transpose(2, 1, 0, 3).reshape(n // 128, 128, k))

    def by_in(w):
        return np.ascontiguousarray(w.reshape(4, 2, 128, 512).transpose(0, 2, 1, 3).reshape(4, 128, 1024))

    def pairs(w):
        return np.ascontiguousarray(w.reshape(4, 128, 4, 2, 128).transpose(2, 1, 3, 0, 4).reshape(4, 128, 1024))

    def feature_major(v):
        return np.ascontiguousarray(v.T.reshape(8, 128, -1).transpose(1, 0, 2))

    vec = np.zeros((128, NV), f)

    def put(name, v):
        lo, hi = COL[name]
        vec[:v.shape[0], lo:hi] = v

    put("g_pre1", cols(x["attn_pre_norm"][0]))
    put("g_post1", cols(x["attn_post_norm"][0]))
    put("g_pre2", cols(x["ffn_pre_norm"][0]))
    put("g_post2", cols(x["ffn_post_norm"][0]))
    put("subln", cols(x["diff_subln"][0]))
    put("sbn", np.concatenate([x["sb_norm"][0]] * 2)[:, None])
    put("lam", np.stack([x["lambda_q1"][0], x["lambda_q2"][0], x["lambda_k1"][0], x["lambda_k2"][0]], axis=1))
    put("table", np.concatenate([x["rel_bias"], np.full((1, 4), NEG, f)]))
    put("sink", np.broadcast_to(x["sink_2"][0][None, :], (128, 8)))
    put("cw", cols(x["conv_w"][0]))
    put("cb", cols(x["conv_b"][0]))
    put("c", np.stack([cols(x["c_2"][0]), cols(x["c_ctx_2"])], axis=2).reshape(128, 16))
    put("bmod", cols(x["b_mod_2"][0]))
    for n, s in (("h_pre1", "g_pre1_2"), ("h_post1", "g_post1_2"), ("h_pre2", "g_pre2_2"), ("h_post2", "g_post2_2")):
        put(n, cols(x[s][0]))
    put("dw", cols(x["conv_w_2"][0]))
    put("db", cols(x["conv_b_2"][0]))

    consts, onehot, rope, dft = _shapes_only()
    qkv = x["w_qkv"][0]
    win = x["w_in_2"][0]
    heads = [0, 4, 1, 5, 2, 6, 3, 7]
    up, up2 = by_out(x["w_up"][0]), by_out(x["w_up_2"][0])
    alt = np.arange(44).reshape(2, 22).T.reshape(44)
    wkv = np.stack([by_out(win[:, 512:640])[0], by_out(win[:, 640:768])[0]])
    arrays = {
        "vec": vec, "consts": consts, "onehot": onehot, "rope": rope,
        "x": feature_major(x["x"][0]), "ctx": feature_major(x["ctx_2"][0]),
        "w_dq": by_out(qkv[:, 0:512]), "w_dk": by_out(qkv[:, 512:1024]), "w_dv": by_in(qkv[:, 1024:1536]),
        "w_sq": by_out(qkv[:, 1536:2048]), "w_sk": by_out(qkv[:, 2048:2560]), "w_sv": by_in(qkv[:, 2560:3072]),
        "w_mod": by_out(x["w_mod_2"][0]), "w_o": by_out(x["w_o"][0]),
        "w_up": up[alt], "w_down": x["w_down"][0].reshape(22, 128, 1024),
        "w_kv2": wkv, "w_q2": by_out(win[:, 0:512].reshape(1024, 8, 64)[:, heads].reshape(1024, 512)),
        "w_f2": by_out(win[:, 768:1280]), "w_g2": by_out(win[:, 1280:3328]), "w_dft": dft,
        "w_pa": pairs(x["w_pa_2"][0].reshape(8, 64, 1024)[heads].reshape(512, 1024)), "w_pf": pairs(x["w_pf_2"][0]),
        "w_out2": by_out(x["w_out_2"][0]), "w_up2": up2[alt], "w_down2": x["w_down_2"][0].reshape(22, 128, 1024),
    }
    nc = _bacc.Bacc("TRN2", target_bir_lowering=False, num_devices=1)
    aps, ins = {}, {}
    for name, v in arrays.items():
        v = np.ascontiguousarray(v)
        ins[f"in_{name}"] = v
        aps[name] = nc.dram_tensor(f"in_{name}", v.shape, mybir.dt.from_np(v.dtype), kind="ExternalInput").ap()
    aps["scratch"] = nc.dram_tensor("bias_rows", [128, 4, 640], mybir.dt.float32, kind="Internal").ap()
    o = nc.dram_tensor("out_x", [128, 8, 512], mybir.dt.float32, kind="ExternalOutput").ap()
    build(nc, aps, o)
    r = _run(nc, [ins], core_ids=[0])
    y = r.results[0]["out_x"]
    return np.ascontiguousarray(y.transpose(1, 0, 2).reshape(1024, 512).T)[None]
```

```python
import math
from collections import namedtuple

import numpy as np

import concourse.bass as bass
from concourse import mybir


T = 512
D = 1024
NF = 22
EPS = 1e-6
LAM_INIT = 0.2
NEG = -1e30
ZCAP = 320.0
SBNEG = -1e5
LN_EXP_SET = 6

_COLS = [
    ("g_pre1", 8), ("g_post1", 8), ("g_pre2", 8), ("g_post2", 8), ("subln", 1), ("sbn", 1), ("lam", 4),
    ("table", 4), ("sink", 8), ("cw", 132), ("cb", 44), ("c", 16), ("bmod", 48),
    ("h_pre1", 8), ("h_post1", 8), ("h_pre2", 8), ("h_post2", 8), ("dw", 66), ("db", 22), ("sel", 2),
]
COL = {}
_at = 0
for _n, _w in _COLS:
    COL[_n] = (_at, _at + _w)
    _at += _w
NV = _at

_CC = [("ident", 128), ("ones", 128), ("tri", 128), ("blk", 128), ("sbmask", 512), ("mlow", 128), ("mhigh", 128),
       ("perm", 128), ("cc", 128), ("sc", 128)]
CCOL = {}
_at = 0
for _n, _w in _CC:
    CCOL[_n] = (_at, _at + _w)
    _at += _w
NC = _at


Token = namedtuple("Token", "sem value")


class Engine:

    def __init__(self, sem):
        self.sem, self.n, self.queue = sem, 0, []

    def op(self, fn, *after, tick=True):
        self.n += tick
        self.queue.append((fn, after, (self.sem, 1) if tick else None))
        return Token(self.sem, self.n) if tick else None

    def dma(self, fn, sem, *after):
        self.queue.append((fn, after, (sem, 16)))

    def run(self, eng):
        waited = {}
        for fn, after, inc in self.queue:
            need, todo = {}, list(after)
            while todo:
                t = todo.pop()
                if isinstance(t, Token):
                    need[t.sem.name] = (t.sem, max(t.value, need.get(t.sem.name, (None, 0))[1]))
                elif t is not None:
                    todo += t
            for name, (sem, value) in need.items():
                if waited.get(name, 0) < value:
                    eng.wait_ge(sem, value)
                    waited[name] = value
            ins = fn()
            if inc:
                ins.then_inc(*inc)


def build(nc, a, out):
    f32, f32r, bf16 = mybir.dt.float32, mybir.dt.float32r, mybir.dt.bfloat16
    ALU, ACT, AX = mybir.AluOpType, mybir.ActivationFunctionType, mybir.AxisListType
    V, S, G, E = nc.vector, nc.scalar, nc.gpsimd, nc.tensor

    base = (nc.sbuf_base + 31) // 32 * 32
    R = {}
    for name, size in [("H", 32768), ("A", 49152), ("M", 32768), ("X", 16384), ("RAW", 20480), ("HL", 40960),
                       ("G", 12288), ("K", 7744)]:
        R[name] = base
        base += size
    assert base <= nc.sbuf_usable_end, base

    def at(name, region, off, shape, dt=f32):
        return nc.alloc_sbuf_tensor_at(name, shape, dt, offset=R[region] + off).ap()

    Hhi = at("Hhi", "H", 0, [128, 8, T], f32r)
    Hlo = at("Hlo", "H", 16384, [128, 8, T], f32r)
    X = at("X", "X", 0, [128, 8, T])
    raw = [at(f"raw{i}", "RAW", 4096 * i, [128, 1024]) for i in range(5)]
    whi = [at(f"whi{i}", "HL", 8192 * i, [128, 1024], f32r) for i in range(5)]
    wlo = [at(f"wlo{i}", "HL", 8192 * i + 4096, [128, 1024], f32r) for i in range(5)]
    vec = at("vec", "K", 0, [128, NV])
    kk = (NV * 4 + 31) // 32 * 32
    ident = at("ident", "K", kk, [128, 128])
    ones = at("ones", "K", kk + 512, [128, 128])
    tri = at("tri", "K", kk + 1024, [128, 128])
    blk = at("blk", "K", kk + 1536, [128, 128])
    sbmask = at("sbmask", "K", kk + 2048, [128, 512])
    identb = at("identb", "K", kk + 4096, [128, 128], bf16)
    mlowb = at("mlowb", "K", kk + 4352, [128, 128], bf16)
    mhighb = at("mhighb", "K", kk + 4608, [128, 128], bf16)
    small = at("small", "K", kk + 4864, [128, 240])
    assert kk + 4864 + 960 <= 7744

    def vc(name, i=0, n=None):
        lo, hi = COL[name]
        return vec[:, lo + i:lo + i + 1] if n is None else vec[:, lo + i:lo + i + n]

    epsc, onec = small[:, 0:1], small[:, 1:2]
    lamc, gd = small[:, 2:3], small[:, 3:4]
    lprod, lexp = small[:, 4:6], small[:, 6:8]
    csil = small[:, 8:24]
    MOD = small[:, 24:120].rearrange("p (j e) -> p j e", e=2)
    G1, G1c, P1, G2, P2 = (small[:, 120 + 8 * i:128 + 8 * i] for i in range(5))
    dmx, dsum, drs, drl = (small[:, 160 + 8 * i:168 + 8 * i].rearrange("p (s e) -> p s e", e=2) for i in range(4))
    amx, anm, asum, ask, atot, arc = (small[:, 192 + 4 * i:196 + 4 * i] for i in range(6))

    PS = nc.alloc_psum_tensor("PS", [128, 8, T], f32).ap()

    def sem(name):
        return nc.alloc_semaphore(name)

    DVE, SCA, PE, POOL, SP = (Engine(sem(n)) for n in ("s_dve", "s_act", "s_pe", "s_pool", "s_sp"))

    def load(queue, name, dst, src, *after):
        s = sem(name)
        queue.dma(lambda: (nc.sync if queue is SP else nc.scalar).dma_start(dst, src), s, *after)
        return Token(s, 16)

    act_set = [None]

    def act(out_, in_, func, *after, bias=0.0, scale=1.0, accum=None):
        if func in (ACT.Exp, ACT.Ln):
            if act_set[0] != LN_EXP_SET:
                act_set[0] = LN_EXP_SET
                SCA.op(lambda: S.add_instruction(mybir.InstLoadActFuncSet(
                    name=nc.get_next_instruction_name(), act_func_set_id=LN_EXP_SET)), tick=False)
        elif func not in (ACT.Copy, ACT.Identity, ACT.Square):
            act_set[0] = func
        kw = {"accum_out": accum} if accum is not None else {}
        return SCA.op(lambda: S.activation(out_, in_, func, bias=bias, scale=scale, **kw), *after)

    def tt(out_, a_, b_, op, *after):
        return DVE.op(lambda: V.tensor_tensor(out_, a_, b_, op), *after)

    def ts(out_, a_, s1, s2, op0, op1, *after):
        return DVE.op(lambda: V.tensor_scalar(out_, a_, s1, s2, op0, op1), *after)

    def stt(out_, a_, s1, b_, op0, op1, *after):
        return DVE.op(lambda: V.scalar_tensor_tensor(out_, a_, s1, b_, op0, op1), *after)

    def pool_tt(out_, a_, b_, op, *after):
        return POOL.op(lambda: G.tensor_tensor(out_, a_, b_, op), *after)

    def mm(out_, l_, r_, start, stop, *after, tick=False, skip=False):
        return PE.op(lambda: E.matmul(out_, l_, r_, start=start, stop=stop, skip_group_check=skip), *after, tick=tick)

    t_vec = load(SP, "l_vec", vec, a["vec"])
    t_ones = load(SP, "l_ones", ones, a["consts"][:, CCOL["ones"][0]:CCOL["ones"][1]])
    onehot = at("onehot", "M", 0, [33, 640])
    t_oh = load(SP, "l_oh", onehot, a["onehot"])

    def load_x(i):
        return load(SP, f"l_x{i}", X[:, 2 * i:2 * i + 2, :], a["x"][:, 2 * i:2 * i + 2, :])

    t_x = [load_x(0)]

    stream = []
    MOD_STREAMED = 9

    def chunks(name, which=None):
        src = a[name]
        for i in (range(src.shape[0]) if which is None else which):
            stream.append(src[i])

    chunks("w_sq"), chunks("w_sk"), chunks("w_sv"), chunks("w_dv"), chunks("w_dq"), chunks("w_dk")
    chunks("w_mod", which=range(4 * MOD_STREAMED))
    chunks("w_o"), chunks("w_up"), chunks("w_down"), chunks("w_kv2")
    chunks("w_q2"), chunks("w_f2"), chunks("w_g2"), chunks("w_dft")
    for i in range(4):
        chunks("w_pa", which=[i])
        chunks("w_pf", which=[i])
    chunks("w_out2"), chunks("w_up2"), chunks("w_down2")

    NR, NH, AHEAD = 5, 5, 4
    s_raw = [sem(f"s_raw{i}") for i in range(NR)]
    raw_done = {}
    hl_free = [None] * NH
    state = {"load": 0, "split": 0, "take": 0, "hl": 0, "pool": ()}
    ready = {}

    def emit_loads(upto=len(stream)):
        while state["load"] < upto:
            i = state["load"]
            if i >= NR and i - NR not in raw_done:
                return
            state["load"] += 1
            SP.dma(lambda i=i: nc.sync.dma_start(raw[i % NR], stream[i]), s_raw[i % NR], raw_done.get(i - NR))

    def landed(i):
        return Token(s_raw[i % NR], 16 * (i // NR + 1))

    def pump(ahead=AHEAD, most=99):
        while state["split"] < min(len(stream), state["take"] + ahead) and most:
            most -= 1
            i = state["split"]
            if i >= state["load"]:
                break
            h = state["hl"] % NH
            if hl_free[h] == "busy":
                break
            r, hi, lo = raw[i % NR], whi[h], wlo[h]
            t_hi = act(hi, r, ACT.Copy, landed(i), hl_free[h])
            sub = pool_tt if i % 2 in state["pool"] else tt
            t_lo = sub(lo, r, hi.bitcast(f32), ALU.subtract, landed(i), hl_free[h], t_hi)
            hl_free[h] = "busy"
            ready[i] = (hi, lo, [t_hi, t_lo], h)
            raw_done[i] = [t_hi, t_lo, landed(i)]
            state["split"] += 1
            state["hl"] += 1
            emit_loads()

    def take(ahead=AHEAD):
        i = state["take"]
        state["take"] += 1
        pump(ahead)
        assert i in ready, i
        hi, lo, tok, h = ready[i]
        return {"i": i, "hi": hi, "lo": lo, "ready": tok, "h": h}

    def release(c, tok, ahead=AHEAD):
        hl_free[c["h"]] = tok
        pump(ahead)

    emit_loads(4)
    t_x += [load_x(i) for i in range(1, 4)]
    emit_loads()

    def const(name, dst, *after):
        lo, hi = CCOL[name]
        return load(SP, "l_" + name, dst, a["consts"][:, lo:hi], *after)

    t_ident, t_tri, t_blk, t_sbmask = (const(n, d) for n, d in (
        ("ident", ident), ("tri", tri), ("blk", blk), ("sbmask", sbmask)))
    t_eps = DVE.op(lambda: V.memset(epsc, EPS))
    t_one = DVE.op(lambda: V.memset(onec, 1.0))
    nsink = small[:, 220:228]
    t_nsink = ts(nsink, vc("sink", n=8), -1.0, 1.0, ALU.mult, ALU.mult, t_vec)

    bank_free = [None] * 8

    def rstd(dst, bank, width, t_stat, dim, *after):
        t = act(dst, PS[:, bank, 0:width], ACT.Ln, t_stat, t_eps, *after, bias=epsc, scale=1.0 / dim)
        bank_free[bank] = t
        return act(dst, dst, ACT.Exp, t, scale=-0.5)

    def cut(hi, lo, v, *after):
        t_hi = act(hi, v, ACT.Copy, *after)
        t_lo = tt(lo, v, hi.bitcast(f32), ALU.subtract, t_hi, *after)
        return [t_hi, t_lo]

    def products(out_, lhs, rhs, first, last, ready_, tick=False):
        mm(out_, lhs[0], rhs[0], first, False, ready_)
        mm(out_, lhs[0], rhs[1], False, False)
        return mm(out_, lhs[1], rhs[0], False, last, tick=tick)

    def wtile(c, k):
        return c["hi"][:, 128 * k:128 * k + 128], c["lo"][:, 128 * k:128 * k + 128]

    def gemm_chunk(c, x, xready, bank, nk=8, off=0, width=T, last_use=True):
        for k in range(nk):
            t = products(PS[:, bank, 0:width], wtile(c, off + k), x(k), k == 0, k == nk - 1,
                         [xready(k), c["ready"], bank_free[bank] if k == 0 else None], tick=k == nk - 1)
        if last_use:
            release(c, t)
        return t

    class Halves:

        def __init__(self, x, xready, bank, done):
            self.c, self.x, self.xready, self.bank, self.done, self.k = None, x, xready, bank, done, 0

        def step(self):
            if self.c is None:
                self.c = take()
            for k in range(self.k, self.k + 4):
                t = products(PS[:, self.bank, :], wtile(self.c, k), self.x(k), k == 0, k == 7,
                             [self.xready(k), self.c["ready"], bank_free[self.bank] if k == 0 else None], tick=k == 7)
            self.k += 4
            if self.k < 8:
                return False
            release(self.c, t)
            self.done(t)
            return True

    def gemm_group(x, xready, banks, cs=None, before=None):
        cs = cs or [take(0) for _ in banks]
        toks = [None] * len(banks)
        for k in range(8):
            if before:
                before(k)
            for j, (c, b) in enumerate(zip(cs, banks)):
                toks[j] = products(PS[:, b, :], wtile(c, k), x(k), k == 0, k == 7,
                                   [xready(k), c["ready"], bank_free[b] if k == 0 else None], tick=k == 7)
        for c, t in zip(cs, toks):
            release(c, t)
        return toks

    def hx(k):
        return Hhi[:, k, :], Hlo[:, k, :]

    G_a = at("G_a", "G", 0, [128, T])
    G_b = at("G_b", "G", 2048, [128, T])
    G_c = at("G_c", "G", 4096, [128, T])
    G_d = at("G_d", "G", 6144, [128, T])
    G_r = at("G_r", "G", 8192, [128, T])
    G_s = at("G_s", "G", 10240, [128, T])

    def normed(src_ready, g, shift, stats_ready, h_free, bank):
        t_r = rstd(G_r, bank, T, stats_ready, D)
        toks, free, last = [], [None, None], None
        for c in range(9):
            if c < 8:
                v = (G_a, G_b)[c % 2]
                t = stt(v, X[:, c, :], g[:, c:c + 1], G_r, ALU.mult, ALU.mult, t_r, free[c % 2], src_ready[c])
                t_hi = act(Hhi[:, c, :], v, ACT.Identity, t, h_free, bias=shift(c))
            if c > 0:
                t_lo = stt(Hlo[:, c - 1, :], (G_a, G_b)[(c - 1) % 2], shift(c - 1), Hhi[:, c - 1, :].bitcast(f32),
                           ALU.add, ALU.subtract, last)
                free[(c - 1) % 2] = [last, t_lo]
                toks.append([last, t_lo])
            last = t_hi
        return toks, [t_r, free]

    class Scaled:

        def __init__(self, g, sq, acc, bank, h_free):
            self.g, self.sq, self.acc, self.bank, self.h_free = g, sq, acc, bank, h_free
            self.sq_free, self.hi, self.tok, self.t_acc = [None] * len(sq), None, [], None

        def begin(self, c, t_in):
            n = c % len(self.sq)
            t_hi = act(Hhi[:, c, :], X[:, c, :], ACT.Identity, t_in, t_vec, self.h_free, scale=self.g[:, c:c + 1])
            sq = self.sq[n] if c else self.acc
            t = act(sq, X[:, c, :], ACT.Square, t_in, self.sq_free[n], self.h_free)
            self.t_acc = pool_tt(self.acc, self.acc, sq, ALU.add, t, self.t_acc) if c else t
            if c:
                self.sq_free[n] = self.t_acc
            self.flush()
            self.hi = (c, t_hi)
            if c == 0:
                self.flush()

        def sum(self):
            self.stat = mm(PS[:, self.bank, :], ones, self.acc, True, True, self.t_acc, t_ones, bank_free[self.bank],
                           tick=True)

        def flush(self):
            if self.hi:
                c, t_hi = self.hi
                t_lo = stt(Hlo[:, c, :], X[:, c, :], self.g[:, c:c + 1], Hhi[:, c, :].bitcast(f32), ALU.mult,
                           ALU.subtract, t_hi)
                self.tok.append([t_hi, t_lo])
                self.hi = None

    t = act(csil, vc("c", n=16), ACT.Silu, t_vec)
    t_csil = t
    t = DVE.op(lambda: V.tensor_tensor(lprod, vc("lam", n=2), vc("lam", 2, n=2), ALU.mult), t_vec)
    t = mm(PS[:, 1, 0:2], ones, lprod, True, True, t, t_ones, bank_free[1], tick=True)
    t = act(lexp, PS[:, 1, 0:2], ACT.Exp, t)
    bank_free[1] = t
    t = tt(lamc, lexp[:, 0:1], lexp[:, 1:2], ALU.subtract, t)
    t_lam = ts(lamc, lamc, LAM_INIT, 1.0, ALU.add, ALU.mult, t)
    t_gd = ts(gd, vc("subln"), 1.0 - LAM_INIT, 1.0, ALU.mult, ALU.mult, t_vec)

    tbl = at("tbl", "M", 2560, [33, 4, 128])
    brow = at("brow", "M", 4608, [128, 4, 640])
    t_tbl = [ts(tbl[:, h, :], ones[0:33, :], vec[0:33, COL["table"][0] + h:COL["table"][0] + h + 1], 1.0, ALU.mult,
                ALU.mult, t_vec, t_ones) for h in range(4)]
    t_brow = []

    def bias_row(h):
        mm(PS[:, 6, 0:512], tbl[:, h, :], onehot[:, 0:512], True, True, t_tbl[h], t_oh, bank_free[6])
        t = mm(PS[:, 7, 0:128], tbl[:, h, :], onehot[:, 512:640], True, True, bank_free[7], tick=True)

        def out():
            t1 = act(brow[:, h, 0:512], PS[:, 6, 0:512], ACT.Copy, t)
            t2 = act(brow[:, h, 512:640], PS[:, 7, 0:128], ACT.Copy, t)
            bank_free[6] = bank_free[7] = t2
            t_brow.append(t2)
        return out

    QS, KS, QD, KD = (at(n, "A", 8192 * i, [128, 4, T]) for i, n in enumerate(("QS", "KS", "QD", "KD")))
    VS = at("VS", "A", 32768, [128, 4, T])
    VD = at("VD", "A", 40960, [128, 4, T])

    def evac(dst, src, bank, *after):
        t = act(dst, src, ACT.Copy, *after)
        bank_free[bank] = t
        return t

    r1 = at("r1", "M", 16384, [128, T])
    rtok = small[:, 216:220]
    scaled = Scaled(vc("g_pre1", n=8), (G_a, G_b, G_c, G_d), G_s, 7, None)

    def hr(k):
        return scaled.tok[k]

    def before(k):
        if k < 7:
            scaled.begin(k + 1, t_x[(k + 1) // 2])
        else:
            scaled.flush()

    def evac_r(dst, bank, t):
        t = tt(dst, PS[:, bank, :], r1, ALU.mult, t, t_r1)
        bank_free[bank] = t
        return t

    scaled.begin(0, t_x[0])
    toks = gemm_group(hx, hr, [0, 1, 2, 3], before=before)
    scaled.sum()
    t_h = scaled.tok
    t_gfree = scaled.stat
    t_r1 = rstd(r1, 7, T, scaled.stat, D)
    t_qs = [evac_r(QS[:, j, :], j, toks[j]) for j in range(4)]
    t_ks = []
    for j in range(4):
        b = 4 + j % 2
        row_out = bias_row(j)
        t = gemm_chunk(take(), hx, hr, b)
        row_out()
        t_ks.append(evac_r(KS[:, j, :], b, t))
    t_brow = load(SP, "l_brow", a["scratch"], brow, t_brow)
    for i in range(4):
        t = PE.op(lambda i=i: E.transpose(PS[:, 7, 128 * i:128 * i + 128], r1[:, 128 * i:128 * i + 128], ident),
                  t_r1, t_ident, bank_free[7])
    t_rtok = ts(rtok, PS[:, 7, :].rearrange("p (a b) -> p a b", b=128)[:, :, 0], 1.0, 1.0, ALU.mult, ALU.mult, t)
    bank_free[7] = t_rtok

    def gemm_v(dst, banks):
        for kc in range(4):
            c = take()
            for j in range(2):
                k = 2 * kc + j
                w = (c["hi"][:, 512 * j:512 * j + 512], c["lo"][:, 512 * j:512 * j + 512])
                for tq in range(4):
                    x = (Hhi[:, k, 128 * tq:128 * tq + 128], Hlo[:, k, 128 * tq:128 * tq + 128])
                    t = products(PS[:, banks[tq], :], x, w, k == 0, k == 7,
                                 [c["ready"], bank_free[banks[tq]] if k == 0 else None], tick=(k == 7 or tq == 3))
                    if k == 7:
                        yield_t[tq] = t
            release(c, t)
        toks = []
        for tq in range(4):
            toks.append(act(dst[:, tq, :], PS[:, banks[tq], :], ACT.Identity, yield_t[tq], t_rtok,
                            scale=rtok[:, tq:tq + 1]))
            bank_free[banks[tq]] = toks[-1]
        return toks

    yield_t = [None] * 4
    t_vs = gemm_v(VS, [0, 1, 2, 3])

    Mhi = at("Mhi", "M", 0, [128, 8, T], f32r)
    Mlo = at("Mlo", "M", 16384, [128, 8, T], f32r)
    Z = [at(f"Z{i}", "G", 4096 * i, [128, 2, T]) for i in range(3)]
    L0 = at("L0", "X", 0, [128, 2, 512])
    L1 = at("L1", "X", 4096, [128, 2, 384])
    L2 = at("L2", "X", 7168, [128, 2, 256])
    L3 = [at(f"L3{i}", "X", 9216 + 1024 * i, [128, 2, 128]) for i in range(2)]
    lhi = [at("L0hi", "M", 0, [128, 2, 512], f32r), at("L1hi", "M", 4096, [128, 2, 384], f32r),
           at("L2hi", "M", 18432, [128, 2, 256], f32r),
           [at(f"L3{i}hi", "M", 20480 + 1024 * i, [128, 2, 128], f32r) for i in range(2)]]
    llo = [at("L0lo", "X", 0, [128, 2, 512], f32r), at("L1lo", "X", 4096, [128, 2, 384], f32r),
           at("L2lo", "X", 7168, [128, 2, 256], f32r),
           [at(f"L3{i}lo", "X", 9216 + 1024 * i, [128, 2, 128], f32r) for i in range(2)]]
    trir = at("trir", "M", 22528, [128, 128], f32r)
    onesr = at("onesr", "M", 23040, [128, 128], f32r)
    t_tr = [act(trir, tri, ACT.Copy, t_tri), act(onesr, ones, ACT.Copy, t_ones)]
    sbr = at("sbr", "X", 11264, [128, T])
    sbt = at("sbt", "X", 13312, [128, T])
    z_free = [t_gfree] * 3
    l_free = {k: t_h for k in ("L0", "L1", "L2", "L30", "L31")}
    x_scratch_done = []
    sbn_free = [t_h, t_h]
    t_mix = [None] * 8
    mix_free = [t_brow]

    def lparts(j, kb):
        return (lhi[3][j % 2], llo[3][j % 2]) if kb == 3 else (lhi[kb], llo[kb])

    def lbuf(j, kb):
        return [L0, L1, L2, L3[j % 2]][kb], ["L0", "L1", "L2", f"L3{j % 2}"][kb]

    def hcx(k):
        return HChi[:, k, :], HClo[:, k, :]

    def head_out(bank_o, t_o, r, v, free):
        t_q = act(r, PS[:, bank_o, :], ACT.Square, t_o, free[0])
        t_v = act(v, PS[:, bank_o, :], ACT.Copy, t_o, free[1])
        bank_free[bank_o] = t_v
        return t_q, t_v

    def head_norm(toks, sbank, weight, dim, gcol, hi, lo, r, v, free, *after):
        t_q, t_v = toks
        t = mm(PS[:, sbank, :], weight, r, True, True, t_q, bank_free[sbank], t_blk, tick=True)
        t_r = rstd(r, sbank, T, t, dim, t)
        free[0] = t = stt(v, v, gcol, r, ALU.mult, ALU.mult, t_r, t_v)
        tk = cut(hi, lo, v, t, *after)
        free[1] = tk
        return tk

    late = []

    sb = {}
    t_lastl = []

    def sb1(s):
        j, kb = s // 4, 3 - s % 4
        w = T - 128 * kb
        z = Z[s % 3]
        for e in range(2):
            p = slice(64 * e, 64 * e + 64)
            t = mm(PS[:, e, 0:w], KS[p, j, 128 * kb:128 * kb + 128], QS[p, j, 128 * kb:T], True, True,
                   bank_free[e], t_ks[j], t_qs[j], tick=True)
        t = stt(z[:, :, 0:w], PS[:, 0:2, 0:w], ZCAP, sbmask[:, None, 0:w].to_broadcast([128, 2, w]), ALU.min, ALU.add,
                t, t_sbmask, z_free[s % 3])
        bank_free[0] = bank_free[1] = t
        lb, name = lbuf(j, kb)
        t_e = act(lb, z[:, :, 0:w], ACT.Exp, t, l_free[name], scale=0.125)
        t_l = act(lb, lb, ACT.Ln, t_e, t_one, bias=onec)
        hi, lo = lparts(j, kb)
        t_hi = act(hi, lb, ACT.Copy, t_l, l_free[name], t_brow)
        sb[s] = [t, t_e, t_hi]

    def sb1b(s):
        j, kb = s // 4, 3 - s % 4
        hi, lo = lparts(j, kb)
        t_hi = sb[s][2]
        sb[s][2] = [t_hi, tt(lo, lbuf(j, kb)[0], hi.bitcast(f32), ALU.subtract, t_hi)]

    def sb2(s):
        j, kb = s // 4, 3 - s % 4
        w = T - 128 * kb
        z = Z[s % 3]
        for e in range(2):
            for i in range(2):
                t = mm(PS[:, 2 + e, 0:w], trir, lparts(j, kb)[i][:, e, :], i == 0, kb == 3 and i == 1, sb[s][2],
                       bank_free[2 + e], t_tr, tick=True)
            for jb in range(kb + 1, 4):
                o = 128 * (jb - kb)
                for i in range(2):
                    t = mm(PS[:, 2 + e, o:w], onesr, lparts(j, jb)[i][:, e, :], False, jb == 3 and i == 1, tick=True)
        if kb == 0:
            for n in range(4):
                l_free[lbuf(j, n)[1]] = t
            t_lastl[:] = [t]
        t_a = stt(z[:, :, 0:w], z[:, :, 0:w], 0.125, PS[:, 2:4, 0:w], ALU.mult, ALU.subtract, t, sb[s][1])
        bank_free[2] = bank_free[3] = t_a
        sb[s] = act(z[:, :, 0:w], z[:, :, 0:w], ACT.Exp, t_a)

    def sb3(s):
        j, kb = s // 4, 3 - s % 4
        w = T - 128 * kb
        z = Z[s % 3]
        for e in range(2):
            t = mm(PS[64 * e:64 * e + 64, 4, 128 * kb:T], VS[:, kb, 128 * j + 64 * e:128 * j + 64 * e + 64],
                   z[:, e, 0:w], kb == 3, kb == 0, sb[s], t_vs[kb], bank_free[4] if kb == 3 else None,
                   tick=True, skip=True)
        z_free[s % 3] = t
        if kb == 0:
            toks = head_out(4, t, sbr, sbt, sbn_free)

            def rest():
                t_mix[4 + j] = head_norm(toks, 5, blk, 64, vc("sbn"), Mhi[:, 4 + j, :], Mlo[:, 4 + j, :], sbr, sbt,
                                         sbn_free, mix_free[0])
                x_scratch_done[:] = [t_mix[4 + j], sbn_free[0]]
            late.append(rest)

    t_qd, t_kd = [], []

    def qk_half(n):
        b = 6 + n % 2

        def done(t):
            if n < 4:
                t_qd.append(evac_r(QD[:, n, :], b, t))
            else:
                t_kd.append(evac_r(KD[:, n - 4, :], b, t))
        return Halves(hx, hr, b, done)

    sb1(0)
    sb1b(0)
    t_vd = gemm_v(VD, [4, 5, 6, 7])
    halves = [qk_half(n) for n in range(8)]

    def sb_step(tick):
        if tick < 16:
            if tick:
                sb1(tick)
            if halves[0].step():
                halves.pop(0)
        while late:
            late.pop()()
        if tick >= 2:
            sb3(tick - 2)
        if 1 <= tick < 17:
            sb2(tick - 1)
        if 1 <= tick < 16:
            sb1b(tick)

    for tick in range(16):
        sb_step(tick)
    t_hfree = Token(PE.sem, PE.n)
    t_sbmask_free = Token(DVE.sem, DVE.n)

    BW = at("BW", "H", 0, [128, 4, 512])
    DL = [at(f"DL{i}", "H", 8192 + 4096 * i, [128, 2, 512]) for i in range(3)]
    DW = [at(f"DW{i}", "H", 20480 + 2048 * i, [128, 512]) for i in range(2)]
    DT = [at(f"DT{i}", "H", 24576 + 2048 * i, [128, 512]) for i in range(2)]
    dnr = at("dnr", "H", 28672, [128, T])
    dnv = at("dnv", "H", 30720, [128, T])
    win = bass.AP(tensor=a["scratch"].tensor, offset=127, ap=[[4 * 640 - 1, 128], [640, 4], [1, 512]])
    t_bw = load(SP, "l_bw", BW, win, t_brow, t_hfree)
    dl_free, dw_free, dt_free, dn_free = [t_hfree] * 3, [t_hfree] * 2, [t_hfree] * 2, [t_hfree, t_hfree]
    df = {}

    def d1(s):
        h, qb = s // 4, s % 4
        n = 128 * (qb + 1)
        l, b = DL[s % 3], 2 * (s % 2)
        for e in range(2):
            p = slice(64 * e, 64 * e + 64)
            t = mm(PS[:, b + e, 0:n], QD[p, h, 128 * qb:128 * qb + 128], KD[p, h, 0:n], True, True, bank_free[b + e],
                   t_qd[h], t_kd[h], tick=True)
        t = stt(l[:, :, 0:n], PS[:, b:b + 2, 0:n], 0.125, BW[:, h:h + 1, 512 - n:512].to_broadcast([128, 2, n]),
                ALU.mult, ALU.add, t, t_bw, dl_free[s % 3])
        bank_free[b] = bank_free[b + 1] = t
        m, sm = dmx[:, s % 4, :], dsum[:, s % 4, :]
        t_m = DVE.op(lambda: V.tensor_reduce(m, l[:, :, 0:n], AX.X, ALU.max, negate=True), t)
        df[s] = t_m

    def d1b(s):
        n = 128 * (s % 4 + 1)
        l, m, sm = DL[s % 3], dmx[:, s % 4, :], dsum[:, s % 4, :]
        for e in range(2):
            t_e = act(l[:, e, 0:n], l[:, e, 0:n], ACT.Exp, df[s], bias=m[:, e:e + 1], accum=sm[:, e:e + 1])
        df[s] = t_e

    def d2(s):
        n = 128 * (s % 4 + 1)
        l, w, q = DL[s % 3], DW[s % 2], s % 4
        t = DVE.op(lambda: V.reciprocal(drs[:, q, :], dsum[:, q, :]), df[s])
        t = tt(drl[:, q, 0:1], drs[:, q, 1:2], lamc, ALU.mult, t, t_lam)
        t = ts(w[:, 0:n], l[:, 1, 0:n], drl[:, q, 0:1], 1.0, ALU.mult, ALU.mult, t, dw_free[s % 2])
        t = stt(w[:, 0:n], l[:, 0, 0:n], drs[:, q, 0:1], w[:, 0:n], ALU.mult, ALU.subtract, t)
        dl_free[s % 3] = df[s] = t

    def d3(s):
        nb = s % 4 + 1
        w, wt = DW[s % 2], DT[s % 2]
        for i in range(nb):
            t = PE.op(lambda i=i: E.transpose(PS[:, 4, 128 * i:128 * i + 128], w[:, 128 * i:128 * i + 128], ident),
                      df[s], t_ident, bank_free[4])
        dw_free[s % 2] = t
        t = evac(wt[:, 0:128 * nb], PS[:, 4, 0:128 * nb], 4, t, dt_free[s % 2])
        df[s] = t

    def d4(s):
        h, qb = s // 4, s % 4
        wt = DT[s % 2]
        for i in range(qb + 1):
            t = mm(PS[:, 5, 128 * qb:128 * qb + 128], VD[:, i, 128 * h:128 * h + 128], wt[:, 128 * i:128 * i + 128],
                   i == 0, i == qb, df[s], t_vd[i], bank_free[5] if qb == 0 else None, tick=True)
        dt_free[s % 2] = t
        if qb == 3:
            toks = head_out(5, t, dnr, dnv, dn_free)

            def rest():
                t_mix[h] = head_norm(toks, 7, ones, 128, gd, Mhi[:, h, :], Mlo[:, h, :], dnr, dnv, dn_free, t_gd,
                                     mix_free[0], t_qd, t_kd, t_lastl)
            late.append(rest)

    cx = at("cx", "A", 0, [128, 160], f32r)
    cx4 = cx[:, 0:32].rearrange("p (k e) -> p k e", e=4)
    csil2 = csil.rearrange("p (k e) -> p k e", e=2)
    t = act(cx[:, 32:160], ones, ACT.Copy, t_hfree, t_ones, scale=0.0)
    t_chi = act(cx4[:, :, 0:2], csil2, ACT.Copy, t_hfree, t_csil)
    t_cx = [t, t_chi, tt(cx4[:, :, 2:4], csil2, cx4[:, :, 0:2].bitcast(f32), ALU.subtract, t_chi)]
    mrow = at("mrow", "K", kk + 2048, [4, 512])
    mod = {"n": 0, "row_free": t_sbmask_free, "t": [None] * 12}

    def mod_row(rows, bank, t):
        t = act(mrow[0:rows, :], PS[0:rows, bank, :], ACT.Copy, t, mod["row_free"])
        bank_free[bank] = t
        return t

    def mod_columns(g, rows, tbank, t_row):
        for n in range(4):
            t = mm(PS[:, tbank, 2 * n:2 * n + 2], mrow[0:rows, 128 * n:128 * n + 128],
                   vec[0:rows, COL["sel"][0]:COL["sel"][1]], True, True, t_row, bank_free[tbank], tick=True)
        mod["row_free"] = t
        t = tt(MOD[:, 4 * g:4 * g + 4, :], PS[:, tbank, 0:8].rearrange("p (j e) -> p j e", e=2),
               vc("bmod", 4 * g, n=4).unsqueeze(2).to_broadcast([128, 4, 2]), ALU.add, t)
        bank_free[tbank] = mod["t"][g] = t

    def mod_chunk():
        g, i = mod["n"] // 4, mod["n"] % 4
        mod["n"] += 1
        c = take()
        for j in range(2):
            k = 2 * i + j
            w = cx[:, 4 * k:4 * k + 128]
            mm(PS[:, 6, :], w, c["hi"][:, 512 * j:512 * j + 512], k == 0, False, c["ready"], t_cx,
               bank_free[6] if k == 0 else None)
            t = mm(PS[:, 6, :], w, c["lo"][:, 512 * j:512 * j + 512], False, k == 7, tick=True)
        release(c, t)
        if i == 1 and g:
            mod_columns(g - 1, 4, 7, mod["row"])
        if i == 3:
            mod["row"] = mod_row(4, 6, t)

    class ModGroup:

        def __init__(self, g, region, off, *free):
            self.g, self.w = g, at(f"mw{g}", region, off, [128, 4, 1024])
            self.t = load(SP, f"l_mw{g}", self.w, a["w_mod"][4 * g:4 * g + 4].rearrange("c p n -> p c n"), *free)

        def run(self, ks, bank):
            for k in ks:
                t = mm(PS[0:2, bank, :], csil[:, 2 * k:2 * k + 2], self.w[:, k // 2, 512 * (k % 2):512 * (k % 2) + 512],
                       k == 0, k == 7, self.t, t_csil, bank_free[bank] if k == 0 else None, tick=True)
            self.done = t

        def row(self, bank):
            self.t_row = mod_row(2, bank, self.done)

        def columns(self, tbank):
            mod_columns(self.g, 2, tbank, self.t_row)

    state["pool"] = (0,)
    for tick in range(20):
        if tick < 2:
            sb_step(16 + tick)
        if 1 <= tick < 17:
            d2(tick - 1)
        if tick < 16:
            d1(tick)
        for _ in range(2):
            if mod["n"] < 4 * MOD_STREAMED:
                mod_chunk()
        if tick < 16:
            d1b(tick)
        if 2 <= tick < 18:
            d3(tick - 2)
        while late:
            late.pop()()
        if 3 <= tick < 19:
            d4(tick - 3)
    state["pool"] = ()
    while mod["n"] < 4 * MOD_STREAMED:
        mod_chunk()
    mod_columns(MOD_STREAMED - 1, 4, 7, mod["row"])
    t_atfree = Token(PE.sem, PE.n)
    t_xback = load(SP, "l_xback", X, a["x"], x_scratch_done, t_atfree)
    mod_group = ModGroup(9, "H", 16384, t_atfree, dl_free, dn_free)

    t = stt(G1, MOD[:, 8:16, 0], 1.0, vc("h_pre1", n=8), ALU.add, ALU.mult, mod["t"][:4])
    t_g1 = stt(G1c, MOD[:, 8:16, 1], 1.0, vc("h_pre1", n=8), ALU.add, ALU.mult, t)
    t_p1 = tt(P1, MOD[:, 16:24, 0], vc("h_post1", n=8), ALU.mult, mod["t"][4:6])

    Y_A = at("Y_A", "A", 0, [128, 8, T])
    Y_M = at("Y_M", "M", 0, [128, 8, T])

    class Post:

        def __init__(self, y, y_free, *after):
            self.y, self.y_free, self.after = y, y_free, after
            self.t_y, self.t_acc, self.sqf = [], None, [None, None]

        def chunk(self, c, bank, t):
            sq = G_s if c == 0 else (G_a, G_b)[c % 2]
            t_q = act(sq, PS[:, bank, :], ACT.Square, t, self.sqf[c % 2], self.after)
            t_y = act(self.y[:, c, :], PS[:, bank, :], ACT.Copy, t, self.y_free)
            bank_free[bank] = t_y
            if c == 0:
                self.t_acc = t_q
            else:
                self.t_acc = self.sqf[c % 2] = tt(G_s, G_s, sq, ALU.add, t_q, self.t_acc)
            self.t_y.append(t_y)

        def rstd(self, bank, group=None, mbank=5):
            if group:
                group.run(range(2), mbank)
            t = mm(PS[:, bank, :], ones, G_s, True, True, self.t_acc, bank_free[bank], tick=True)
            self.t_r = rstd(G_r, bank, T, t, D)
            if group:
                group.run(range(2, 8), mbank)
            self.vf = [self.sqf, self.sqf]
            self.toks = []

        def residual(self, c, g, x_ready, odd=pool_tt):
            v = (G_a, G_b)[c % 2]
            mul = odd if c % 2 else tt
            t = mul(v, self.y[:, c, :], G_r, ALU.mult, self.t_r, self.t_y[c], self.vf[c % 2])
            t = self.vf[c % 2] = stt(X[:, c, :], v, g[:, c:c + 1], X[:, c, :], ALU.mult, ALU.add, t, x_ready)
            self.toks.append(t)
            return t

        def squared(self, c, bank, sqs, sqf):
            sq = sqs[c % 4]
            t = act(sq, X[:, c, :], ACT.Square, self.toks[c], sqf[c % 4])
            sqf[c % 4] = mm(PS[:, bank, :], ones, sq, c == 0, c == 7, t, bank_free[bank] if c == 0 else None,
                            tick=True)
            return sqf[c % 4]

    outs = []

    post = Post(Y_A, t_atfree, z_free)
    for o in range(8):
        b = o % 5

        def mixt(k):
            k = (4, 5, 6, 7, 0, 1, 2, 3)[k]
            return Mhi[:, k, :], Mlo[:, k, :]

        c = take()
        for i, k in enumerate((4, 5, 6, 7, 0, 1, 2, 3)):
            t = products(PS[:, b, :], wtile(c, k), (Mhi[:, k, :], Mlo[:, k, :]), i == 0, i == 7,
                         [t_mix[k], c["ready"], bank_free[b] if i == 0 else None], tick=i == 7)
        release(c, t)
        post.chunk(o, b, t)
    t_mixfree = t
    post.rstd(7, mod_group)
    pump(4)
    r2 = G_s
    scaled = Scaled(vc("g_pre2", n=8), (G_c, G_d), at("sacc", "M", 6144, [128, T]), 6, [dn_free, t_mixfree, mod_group.done])

    ACTV = at("ACTV", "A", 0, [128, NF, T])
    C = [at(f"C{i}", "M", 2048 * i, [128, T]) for i in range(8)]
    y_free = []
    c_free = [t_mixfree] * 8

    def conv_mid(src, t, buf, tap, bias):
        return act(C[buf], src, ACT.Identity, t, c_free[buf], bias=bias, scale=tap)

    def conv(src, t, buf, taps, shifts):
        dst = C[buf]
        for tap, sh in zip(taps, shifts):
            if sh == 0:
                continue
            if sh < 0:
                o_, i_ = dst[:, -sh:T], src[:, 0:T + sh]
            else:
                o_, i_ = dst[:, 0:T - sh], src[:, sh:T]
            t = stt(o_, i_, tap, o_, ALU.mult, ALU.add, t)
        return t

    act_ready = [None] * NF

    def up1a(n, bank, t):
        f, is_val = n // 2, n % 2
        col = f + NF * is_val
        u = (G_a, G_b)[n % 2]
        t = tt(u, PS[:, bank, :], r2, ALU.mult, t, t_r2, u_free[n % 2])
        bank_free[bank] = t
        return conv_mid(u, t, n % 4, vc("cw", 88 + col), vc("cb", col))

    def up1b(n, bank, t):
        f, is_val = n // 2, n % 2
        col = f + NF * is_val
        u = (G_a, G_b)[n % 2]
        t = conv(u, t, n % 4, [vc("cw", 44 * i + col) for i in range(2)], [-2, -1])
        u_free[n % 2] = t
        if not is_val:
            held[0] = act(C[n % 4], C[n % 4], ACT.Gelu_apprx_tanh, t)
        else:
            t = tt(ACTV[:, f, :], C[(n - 1) % 4], C[n % 4], ALU.mult, t, held[0], y_free)
            c_free[(n - 1) % 4] = c_free[n % 4] = t
            act_ready[f] = t
        if n >= 9 and ctx_steps:
            ctx_steps.pop(0)()

    held = [None]

    d_at = [("M", 8192), ("M", 12288), ("H", 0), ("H", 4096)]
    Dhi = [at(f"Dhi{i}", *d_at[i], [128, T], f32r) for i in range(4)]
    Dlo = [at(f"Dlo{i}", d_at[i][0], d_at[i][1] + 2048, [128, T], f32r) for i in range(4)]
    d_free, d_tok = [None] * 4, {}

    def prep(f):
        d_tok[f] = cut(Dhi[f % 4], Dlo[f % 4], ACTV[:, f, :], act_ready[f], d_free[f % 4])

    def up_phase(first, second, hr_, before=None, after_group=None):
        toks = gemm_group(hx, hr_, [0, 1, 2, 3], before=before)
        if after_group:
            after_group()
        held_back = None
        for n in range(2 * NF):
            b = n if n < 6 else n % 6
            t = toks[n] if n < 4 else gemm_chunk(take(), hx, hr_, b)
            if n in (2 * NF - 5, 2 * NF - 3):
                prep((n - 2 * NF + 5) // 2)
            t = first(n, b, t)
            if held_back:
                second(*held_back)
            held_back = (n, b, t)
        second(*held_back)

    def before(k):
        for c in ((0, 1) if k == 0 else (k + 1,)):
            if c < 8:
                scaled.begin(c, post.residual(c, vc("g_post1", n=8), [t_xback, t_vec], odd=tt))
            else:
                scaled.flush()
        if k == 1:
            mod_group.row(5)
        if k == 7:
            mod_group.columns(4)

    t_r2 = []

    def after_group():
        scaled.sum()
        c_free[3] = [t_mixfree, scaled.stat]
        t_r2.append(rstd(r2, 6, T, scaled.stat, D, post.t_r))
        u_free[:] = [post.vf, post.vf]

    u_free = [None, None]

    Xc = at("Xc", "M", 8192, [128, 8, 256])
    HChi = at("HChi", "M", 16384, [128, 8, 256], f32r)
    HClo = at("HClo", "M", 24576, [128, 8, 256], f32r)
    t_xc = load(SP, "l_xc", Xc, a["ctx"], t_mixfree)
    ctx = {"free": [None, None], "hc": [], "sq": []}

    def ctx_sum(last=False):
        if len(ctx["sq"]) > 1 or last:
            c, v, t = ctx["sq"].pop(0)
            ctx["stat"] = ctx["free"][c % 2] = mm(PS[:, 7, 0:256], ones, v, c == 0, c == 7, t,
                                                  bank_free[7] if c == 0 else None, tick=True)

    def ctx_square(c):
        ctx_sum()
        v = (G_c, G_d)[c % 2][:, 0:256]
        t = act(v, Xc[:, c, :], ACT.Square, t_xc, ctx["free"][c % 2], scaled.sq_free)
        ctx["sq"].append((c, v, t))

    def ctx_rstd():
        ctx_sum(True)
        ctx_sum(True)
        ctx["r"] = rstd(G_r[:, 0:256], 7, 256, ctx["stat"], D, post.toks)

    def ctx_norm(c):
        v = (G_c, G_d)[c % 2][:, 0:256]
        t = pool_tt(v, Xc[:, c, :], G_r[:, 0:256], ALU.mult, ctx["r"], ctx["free"][c % 2])
        t = act(v, v, ACT.Identity, t, t_g1, scale=G1c[:, c:c + 1], bias=MOD[:, c, 1:2])
        t_hi = act(HChi[:, c, :], v, ACT.Copy, t)
        ctx["free"][c % 2] = [t_hi, pool_tt(HClo[:, c, :], v, HChi[:, c, :].bitcast(f32), ALU.subtract, t_hi)]
        ctx["hc"].append(ctx["free"][c % 2])

    ctx_steps = [lambda c=c: ctx_square(c) for c in range(8)] + [lambda: None, ctx_rstd] + [lambda c=c: ctx_norm(c) for c in range(8)]
    d_free[0:2] = [ctx["hc"]] * 2
    up_phase(up1a, up1b, lambda k: scaled.tok[k], before, after_group)
    t_x1 = post.toks
    y_free.append(t_x1)
    t_upfree = Token(PE.sem, PE.n)

    def down_phase(post):
        d_free[2:] = [t_upfree] * 2
        prep(2)
        tail = 2
        for f in range(NF - tail):
            if f + 3 < NF:
                prep(f + 3)
            c = take()
            for i, o in enumerate((6, 7, 2, 3, 4, 5, 0, 1)):
                t = products(PS[:, o, :], wtile(c, o), (Dhi[f % 4], Dlo[f % 4]), f == 0, False,
                             [d_tok[f], c["ready"], bank_free[o] if f == 0 else None], tick=i == 7)
            release(c, t)
            d_free[f % 4] = t
        post.y_free = [d_tok[f] for f in range(8)]
        cs = [take() for _ in range(tail)]
        for o in range(8):
            for i, c in enumerate(cs):
                f = NF - tail + i
                t = products(PS[:, o, :], wtile(c, o), (Dhi[f % 4], Dlo[f % 4]), False, i == tail - 1,
                             [d_tok[f], c["ready"]], tick=i == tail - 1)
            post.chunk(o, o, t)
        for c in cs:
            release(c, t, 0)
        return t

    mod_group = ModGroup(10, "H", 16384, t_upfree)
    post = Post(Y_A, None, u_free)
    t_down = down_phase(post)
    post.rstd(0, mod_group, 1)
    sqs = [G_c, G_d, at("sq2", "M", 0, [128, T]), at("sq3", "M", 2048, [128, T])]
    sqf = [ctx["free"], ctx["free"], c_free, c_free]
    cK, cV = take(0), take(0)
    for c in range(8):
        post.residual(c, vc("g_post2", n=8), [t_x1])
        t_stat = post.squared(c, 3, sqs, sqf)
        if c == 1:
            mod_group.row(1)
            t_kc = gemm_chunk(cK, hcx, lambda k: ctx["hc"][k], 4, width=256, last_use=False)
        if c == 7:
            state["pool"] = (0, 1)
            pump(3, 1)
            state["pool"] = ()
    mod_group.columns(2)
    for tq in range(2):
        for k in range(8):
            x = (HChi[:, k, 128 * tq:128 * tq + 128], HClo[:, k, 128 * tq:128 * tq + 128])
            t = products(PS[:, 5, 128 * tq:128 * tq + 128], x, wtile(cV, k), k == 0, k == 7,
                         [cV["ready"], bank_free[5] if k + tq == 0 else None], tick=k == 7)
    t_vc = t_hcfree = t
    pump(3, 1)
    t_x2 = post.toks
    t_h, t_gf = normed(t_x2, G1, lambda c: MOD[:, c, 0:1], t_stat, [t_down, t_g1, mod_group.done], 3)
    t_g2 = stt(G2, MOD[:, 32:40, 0], 1.0, vc("h_pre2", n=8), ALU.add, ALU.mult, mod["t"][8:10])
    t_gf2 = [t_gf, sqf]

    Q2 = at("Q2", "A", 0, [128, 4, T])
    K2 = at("K2", "A", 8192, [128, T])
    V2 = at("V2", "A", 10240, [128, 4, 128])
    KC = at("KC", "A", 12288, [128, 256])
    VC = at("VC", "A", 13312, [128, 2, 128])
    Fhi = at("Fhi", "A", 14336, [128, 4, T], f32r)
    Flo = at("Flo", "A", 22528, [128, 4, T], f32r)
    AThi = at("AThi", "A", 30720, [128, 4, T], f32r)
    ATlo = at("ATlo", "A", 38912, [128, 4, T], f32r)
    ropeC = at("ropeC", "G", 8192, [128, T])
    ropeS = at("ropeS", "G", 10240, [128, T])
    a_free = [t_down, t_x2]
    hr2 = lambda k: t_h[k]

    t_kc = evac(KC, PS[:, 4, 0:256], 4, t_kc, a_free)
    t_v2 = [evac(VC, PS[:, 5, 0:256].rearrange("p (a b) -> p a b", a=2), 5, t_vc, a_free)]
    toks = gemm_group(hx, hr2, [0, 1, 2, 3], cs=[cK, take(0), take(0), take(0)])

    permc = at("permc", "M", 28672, [128, 128])
    t_perm = load(SP, "l_perm", permc, a["consts"][:, CCOL["perm"][0]:CCOL["perm"][1]], [t_hcfree])
    t_rc = load(SP, "l_rc", ropeC, a["rope"][:, 0, :], [t_h, t_gf2])
    t_rs = load(SP, "l_rs", ropeS, a["rope"][:, 1, :], [t_h, t_gf2])
    rt = [t_gf2]

    def rope(x, t_x):
        t = mm(PS[:, 5, :], permc, x, True, True, t_x, t_perm, bank_free[5], tick=True)
        t2 = tt(G_b, PS[:, 5, :], ropeS, ALU.mult, t, t_rs, rt[0])
        bank_free[5] = t2
        t3 = tt(x, x, ropeC, ALU.mult, t, t_rc)
        rt[0] = tt(x, x, G_b, ALU.add, t2, t3)
        return rt[0]

    def v_part(tq):
        b = 4 + tq % 2 * 3
        for k in range(8):
            x = (Hhi[:, k, 128 * tq:128 * tq + 128], Hlo[:, k, 128 * tq:128 * tq + 128])
            t = products(PS[:, b, 0:128], x, wtile(cV, k), k == 0, k == 7,
                         [cV["ready"], bank_free[b] if k == 0 else None], tick=k == 7)
        if tq == 3:
            release(cV, t)
        t_v2.append(evac(V2[:, tq, :], PS[:, b, 0:128], b, t, a_free))

    bmf = at("bmf", "M", 29184, [128, 2, 128])
    t_bm = load(SP, "l_bm", bmf, a["consts"][:, CCOL["mlow"][0]:CCOL["mhigh"][1]].rearrange("p (a b) -> p a b", a=2),
                [t_hcfree])
    t1 = ts(mlowb, bmf[:, 0, :], 1.0, 1.0, ALU.mult, ALU.mult, t_bm)
    t2 = ts(mhighb, bmf[:, 1, :], 1.0, 1.0, ALU.mult, ALU.mult, t_bm)
    t3 = ts(identb, ident, 1.0, 1.0, ALU.mult, ALU.mult, t_ident)
    t_masks = [t1, t2, t3]
    ccs = at("ccs", "M", 31744, [128, 256])
    cchi = at("cchi", "K", kk + 2048, [128, 256], f32r)
    cclo = at("cclo", "K", kk + 3072, [128, 256], f32r)
    t_ccs = load(SP, "l_ccs", ccs, a["consts"][:, CCOL["cc"][0]:CCOL["sc"][1]], t_hcfree)
    t_cc = []
    t_k2 = evac(K2, PS[:, 0, :], 0, toks[0], a_free)
    t_q2 = [evac(Q2[:, j, :], PS[:, 1 + j, :], 1 + j, toks[1 + j], a_free) for j in range(3)]
    v_part(0)
    v_part(1)
    t_k2 = rope(K2, t_k2)
    v_part(2)
    t_q2[0] = rope(Q2[:, 0, :], t_q2[0])
    v_part(3)
    t_q2[1] = rope(Q2[:, 1, :], t_q2[1])
    t = gemm_chunk(take(), hx, hr2, 6)
    t_q3 = evac(Q2[:, 3, :], PS[:, 6, :], 6, t)
    t_q2[2] = rope(Q2[:, 2, :], t_q2[2])

    GT = at("GT", "M", 0, [128, 16, T])
    t_f, t_g = [], [None] * 16

    def branch(kind, i):
        def done(t):
            if kind == "f":
                t_hi = act(Fhi[:, i, :], PS[:, 7, :], ACT.Copy, t, a_free)
                t_lo = tt(Flo[:, i, :], PS[:, 7, :], Fhi[:, i, :].bitcast(f32), ALU.subtract, t_hi)
                bank_free[7] = t_lo
                t_f.append([t_hi, t_lo])
            else:
                t_g[i] = evac(GT[:, i, :], PS[:, 7, :], 7, t, t_hcfree, rt[0], t_masks, t_cc)
        return Halves(hx, hr2, 7, done)

    halves = [branch("f", i) for i in range(4)] + [branch("g", i) for i in range(16)]
    left = [2 * len(halves)]

    def fill():
        left[0] -= 1
        if halves[0].step():
            halves.pop(0)

    fill()
    t_q2.append(rope(Q2[:, 3, :], t_q3))
    fill()

    P2b = [at(f"P2b{i}", "G", 2560 * i, [128, 640]) for i in range(2)]
    PT2 = [at(f"PT2{i}", "G", 5120 + 2560 * i, [128, 640]) for i in range(2)]
    O2 = [at(f"O2{i}", "G", 10240 + 512 * i, [128, 128]) for i in range(4)]
    OT = [at(f"OT{i}", "A", 47104 + 512 * i, [128, 128]) for i in range(4)]
    g_all = [rt[0], t_k2, t_q2]
    p_free, pt_free, o2_free, ot_free = [g_all] * 2, [g_all] * 2, [g_all] * 4, [a_free] * 4
    at_tok = [[] for _ in range(4)]
    ab = {}

    def geom(s):
        j, qb, e = s // 8, s // 2 % 4, s % 2
        k0, k1 = max(qb - 1, 0), min(qb + 1, 3)
        return j, qb, e, k0, k1 - k0 + 1

    def a1(s):
        j, qb, e, k0, nl = geom(s)
        n, b = 128 * (nl + 2), 2 * (s % 2)
        p = slice(64 * e, 64 * e + 64)
        q = Q2[p, j, 128 * qb:128 * qb + 128]
        flat = PS[:, b:b + 2, :].rearrange("p a b -> p (a b)")
        masks = [(0, mlowb)] * (qb > 0) + [(128 * (nl - 1), mhighb)] * (qb < 3)
        mm(flat[:, 0:128 * nl], q, K2[p, 128 * k0:128 * (k0 + nl)], True, False, bank_free[b], bank_free[b + 1],
           t_q2[j], t_k2, t_kc)
        for i, (o, m) in enumerate(masks):
            t = mm(flat[:, o:o + 128], identb, m, False, i == len(masks) - 1, t_masks)
        if nl == 2:
            t = mm(flat[:, 256:512], q, KC[p, :], True, True, tick=True)
        else:
            mm(flat[:, 384:512], q, KC[p, 0:128], True, True)
            t = mm(flat[:, 512:640], q, KC[p, 128:256], True, True, tick=True)
        i = s % 4
        h = j + 4 * e
        m, sm = amx[:, i:i + 1], asum[:, i:i + 1]
        t_m = DVE.op(lambda: V.tensor_reduce(m, flat[:, 0:n], AX.X, ALU.max, negate=True), t)
        t_m = ts(anm[:, i:i + 1], m, 0.125, nsink[:, h:h + 1], ALU.mult, ALU.min, t_m, t_nsink)
        t_e = act(P2b[s % 2][:, 0:n], flat[:, 0:n], ACT.Exp, t_m, p_free[s % 2], bias=anm[:, i:i + 1], scale=0.125,
                  accum=sm)
        bank_free[b] = bank_free[b + 1] = t_e
        t_s = act(ask[:, i:i + 1], vc("sink", h), ACT.Exp, t_m, bias=anm[:, i:i + 1])
        t = tt(atot[:, i:i + 1], sm, ask[:, i:i + 1], ALU.add, t_e, t_s)
        t = DVE.op(lambda: V.reciprocal(arc[:, i:i + 1], atot[:, i:i + 1]), t)
        ab[s] = [t_e, t]

    def a2(s):
        j, qb, e, k0, nl = geom(s)
        n = nl + 2
        t_e, t_r = ab[s]
        p, pt = P2b[s % 2], PT2[s % 2]
        tp = PS[:, 4:6, :].rearrange("p a b -> p (a b)")
        for i in range(n):
            t = PE.op(lambda i=i: E.transpose(tp[:, 128 * i:128 * i + 128], p[:, 128 * i:128 * i + 128], ident),
                      t_e, t_ident, bank_free[4], bank_free[5])
        p_free[s % 2] = t
        t = evac(pt[:, 0:128 * n], tp[:, 0:128 * n], 4, t, pt_free[s % 2])
        bank_free[5] = t
        ab[s] = [t, t_r]

    def a3(s):
        j, qb, e, k0, nl = geom(s)
        n = nl + 2
        t_pt, t_r = ab[s]
        pt = PT2[s % 2]
        o = PS[:, 6, 64 * (s % 2):64 * (s % 2) + 64]
        for i in range(n):
            v = V2[:, k0 + i, 64 * e:64 * e + 64] if i < nl else VC[:, i - nl, 64 * e:64 * e + 64]
            t = mm(o, pt[:, 128 * i:128 * i + 128], v, i == 0, i == n - 1, t_pt, t_v2, bank_free[6], tick=True)
        pt_free[s % 2] = t
        r = s // 2 % 4
        i = s % 4
        t = ts(O2[r][:, 64 * e:64 * e + 64], o, arc[:, i:i + 1], 1.0, ALU.mult, ALU.mult, t, t_r, o2_free[r])
        bank_free[6] = t
        ab[s] = t

    def a4(s):
        j, qb, e, k0, nl = geom(s)
        if not e:
            return
        r = s // 2 % 4
        q = slice(128 * qb, 128 * qb + 128)
        t = PE.op(lambda: E.transpose(PS[:, 6, 128:256], O2[r], ident), ab[s], ab[s - 1], bank_free[6])
        o2_free[r] = t
        t_o = act(OT[r], PS[:, 6, 128:256], ACT.Copy, t, ot_free[r])
        bank_free[6] = t_o
        ot_free[r] = cut(AThi[:, j, q], ATlo[:, j, q], OT[r], t_o, a_free)
        at_tok[j].append(ot_free[r])

    for tick in range(37):
        if tick == 6:
            t_cc.append(cut(cchi, cclo, ccs, t_ccs, mod["row_free"]))
        if tick < 32:
            a1(tick)
        while halves and left[0] > 38 - (tick + 1) * 38 // 34:
            fill()
        if 3 <= tick < 35:
            a3(tick - 3)
        if 1 <= tick < 33:
            a2(tick - 1)
        if tick >= 5:
            a4(tick - 5)
    t_h2free = Token(PE.sem, PE.n)

    ABhi = at("ABhi", "H", 0, [128, 4, 4, 256], f32r)
    AThi_all = [x for y in at_tok for x in y]
    ABlo = at("ABlo", "H", 16384, [128, 4, 4, 256], f32r)
    t_ab = {}
    n = 0
    for g in range(4):
        for st in range(4):
            b = n % 4
            n += 1
            t = products(PS[:, b, 0:256], (Fhi[:, g, 128 * st:128 * st + 128], Flo[:, g, 128 * st:128 * st + 128]),
                         (cchi, cclo), True, True, [t_f[g], t_cc, bank_free[b]], tick=True)
            t_hi = act(ABhi[:, g, st, :], PS[:, b, 0:256], ACT.Copy, t, t_h2free)
            t_lo = tt(ABlo[:, g, st, :], PS[:, b, 0:256], ABhi[:, g, st, :].bitcast(f32), ALU.subtract, t_hi)
            bank_free[b] = t_lo
            t_ab[g, st] = [t_hi, t_lo]
    mod["row_free"] = t
    FOhi = at("FOhi", "A", 14336, [128, 4, T], f32r)
    FOlo = at("FOlo", "A", 22528, [128, 4, T], f32r)
    cs = [take() for _ in range(4)]
    t_fo, fo_free = [], t
    for g in range(4):
        b = 4 + g % 2
        i = 0
        for trig in range(2):
            for st in range(4):
                c = cs[2 * trig + st // 2]
                w = (c["hi"][:, 512 * (st % 2):512 * (st % 2) + 512], c["lo"][:, 512 * (st % 2):512 * (st % 2) + 512])
                x = (ABhi[:, g, st, 128 * trig:128 * trig + 128], ABlo[:, g, st, 128 * trig:128 * trig + 128])
                t = products(PS[:, b, :], x, w, i == 0, i == 7,
                             [t_ab[g, st], c["ready"], bank_free[b] if i == 0 else None], tick=i == 7)
                i += 1
        t_hi = act(FOhi[:, g, :], PS[:, b, :], ACT.Copy, t, fo_free)
        t_lo = tt(FOlo[:, g, :], PS[:, b, :], FOhi[:, g, :].bitcast(f32), ALU.subtract, t_hi)
        bank_free[b] = t_lo
        t_fo.append([t_hi, t_lo])
    for c in cs:
        release(c, t)
    t_abfree = t

    MGhi = at("MGhi", "H", 0, [128, 8, T], f32r)
    MGlo = at("MGlo", "H", 16384, [128, 8, T], f32r)
    mg_free = [None, None]
    t_sig = [None] * 16
    t_mg = []
    mt = [(at("mt0", "G", 3072, [128, T]), at("mt1", "G", 5120, [128, T])),
          (at("mt2", "G", 7168, [128, T]), at("mt3", "G", 9216, [128, T]))]
    mt_free = [[AThi_all, ot_free], [AThi_all, ot_free]]
    for o2 in range(4):
        ca, cf = take(), take()
        for e in range(2):
            o = 2 * o2 + e
            b = 2 * (o % 3)
            for i in (o, 8 + o):
                t_sig[i] = act(GT[:, i, :], GT[:, i, :], ACT.Sigmoid, t_g[i])
            t_a = gemm_chunk(ca, lambda k: (AThi[:, k, :], ATlo[:, k, :]), lambda k: at_tok[k], b, nk=4, off=4 * e,
                             last_use=e == 1)
            t_b = gemm_chunk(cf, lambda k: (FOhi[:, k, :], FOlo[:, k, :]), lambda k: t_fo[k], b + 1, nk=4, off=4 * e,
                             last_use=e == 1)
            u, v = mt[o % 2]
            ta = tt(u, PS[:, b, :], GT[:, o, :], ALU.mult, t_a, t_sig[o], mt_free[o % 2])
            tb = tt(v, PS[:, b + 1, :], GT[:, 8 + o, :], ALU.mult, t_b, t_sig[8 + o])
            bank_free[b], bank_free[b + 1] = ta, tb
            t = tt(u, u, v, ALU.add, ta, tb)
            mt_free[o % 2] = cut(MGhi[:, o, :], MGlo[:, o, :], u, t, t_abfree)
            t_mg.append(mt_free[o % 2])
    t_gtfree = [t_mg, ta, tb]

    mod_group = ModGroup(11, "A", 14336, t_mg, ta, tb)
    post = Post(Y_M, t_gtfree, t_mg)
    for o in range(8):
        b = (0, 1, 2, 3, 4)[o % 5]
        t = gemm_chunk(take(), lambda k: (MGhi[:, k, :], MGlo[:, k, :]), lambda k: t_mg[k], b)
        post.chunk(o, b, t)
    t_mgfree = t
    post.rstd(7, mod_group)
    sqs[2:] = [at("sq4", "M", 16384, [128, T]), at("sq5", "M", 18432, [128, T])]
    sqf = [t_mg] * 4
    for c in range(8):
        post.residual(c, P1, [t_x2, t_p1])
        t_stat = post.squared(c, 6, sqs, sqf)
        if c == 1:
            mod_group.row(5)
    mod_group.columns(4)
    state["pool"] = (0, 1)
    pump(4, 1)
    state["pool"] = ()
    t_x3 = post.toks
    t_h, t_gf = normed(t_x3, G2, lambda c: MOD[:, 24 + c, 0:1], t_stat, [t_mgfree, t_g2], 6)
    t_p2 = tt(P2, MOD[:, 40:48, 0], vc("h_post2", n=8), ALU.mult, mod["t"][10:12])

    y_free = [t_x3, t_mgfree, t_fo, mod_group.done]
    c_free = [t_x3] * 8

    def up2a(n, bank, t):
        f = n // 2
        return t if n % 2 else conv_mid(PS[:, bank, :], t, f % 4, vc("dw", NF + f), vc("db", f))

    def up2b(n, bank, t):
        f = n // 2
        if n % 2 == 0:
            t = conv(PS[:, bank, :], t, f % 4, [vc("dw", NF * i + f) for i in (0, 2)], [-1, 1])
            bank_free[bank] = t
            held[0] = act(C[f % 4], C[f % 4], ACT.Silu, t)
        else:
            t = tt(ACTV[:, f, :], PS[:, bank, :], C[f % 4], ALU.mult, t, held[0], y_free)
            bank_free[bank] = t
            c_free[f % 4] = t
            act_ready[f] = t

    d_free[0:2] = [t_x3] * 2
    up_phase(up2a, up2b, lambda k: t_h[k])
    t_upfree = Token(PE.sem, PE.n)
    post = Post(Y_A, None, t_gf)
    down_phase(post)
    post.rstd(0)
    for c in range(8):
        t = post.residual(c, P2, [t_x3, t_p2])
        o = sem(f"s_out{c}")
        SP.dma(lambda c=c: nc.sync.dma_start(out[:, c, :], X[:, c, :]), o, t)
        outs.append(Token(o, 16))
    assert state["take"] == len(stream)
    s_end = sem("s_end")
    SP.queue.append((lambda: nc.sync.nop(), tuple(outs), (s_end, 1)))

    with nc.Block() as block:
        @block.sync
        def _(e):
            SP.run(e)

        @block.scalar
        def _(e):
            SCA.run(e)

        @block.vector
        def _(e):
            DVE.run(e)

        @block.gpsimd
        def _(e):
            POOL.run(e)

        @block.tensor
        def _(e):
            PE.run(e)



def _shapes_only():
    i = np.arange(128)
    k, q = i[:, None], i[None, :]
    c = np.zeros((128, NC), np.float32)

    def put(name, v):
        c[:, CCOL[name][0]:CCOL[name][1]] = v

    put("ident", np.eye(128))
    put("ones", 1.0)
    put("tri", k >= q)
    put("blk", (k // 64) == (q // 64))
    m = np.zeros((128, 512))
    m[:, :128] = np.where(k < q, 0.0, SBNEG)
    put("sbmask", m)
    put("mlow", np.where(q >= k, 0.0, NEG))
    put("mhigh", np.where(q <= k, 0.0, NEG))
    d = i % 32
    src = np.where(d < 16, i + 16, i - 16)
    put("perm", (i[:, None] == src[None, :]))
    cc = np.outer(i, i) % 128 * (2 * np.pi / 128)
    norm = 1.0 / math.sqrt(512 * 128)
    put("cc", np.cos(cc))
    put("sc", -np.sin(cc))

    rel = 511 - np.arange(640)
    n = np.maximum(rel, 0)
    nf = np.maximum(n, 1).astype(np.float32)
    large = 16 + (np.log(nf / np.float32(16)) / np.float32(math.log(8)) * np.float32(16)).astype(np.int32)
    bucket = np.where(n < 16, n, np.minimum(large, 31))
    onehot = np.zeros((33, 640), np.float32)
    onehot[bucket, np.arange(640)] = 1.0
    onehot[:, rel < 0] = 0.0
    onehot[32, rel < 0] = 1.0

    t = np.arange(512)
    row, col = (t // 64).astype(np.float32), (t % 64).astype(np.float32)
    inv = (np.float32(10000.0) ** (-np.arange(0, 32, 2, dtype=np.float32) / np.float32(32))).astype(np.float32)
    rope = np.zeros((128, 2, 512), np.float32)
    for p in range(128):
        pos = row if p % 64 < 32 else col
        ang = (pos * inv[p % 16]).astype(np.float32)
        rope[p, 0] = np.cos(ang)
        rope[p, 1] = np.sin(ang) * (-1.0 if p % 32 < 16 else 1.0)

    ang = np.outer(t, t) % 512 * (2 * np.pi / 512)
    dft = np.stack([np.cos(ang) * norm, np.sin(ang) * norm]).astype(np.float32)
    dft = dft.reshape(2, 2, 2, 128, 512).transpose(0, 1, 3, 2, 4).reshape(4, 128, 1024)
    return c, onehot, rope, np.ascontiguousarray(dft)


def kernel(**inputs):
    import concourse.bacc as _bacc
    from concourse.bass_utils import run_bass_kernel_spmd as _run

    x = {k: np.asarray(v) for k, v in inputs.items()}
    f = np.float32

    def cols(v):
        return np.ascontiguousarray(v).reshape(-1, 128).T

    def by_out(w):
        k, n = w.shape
        return np.ascontiguousarray(
            w.reshape(k // 128, 128, n // 128, 128).transpose(2, 1, 0, 3).reshape(n // 128, 128, k))

    def by_in(w):
        return np.ascontiguousarray(w.reshape(4, 2, 128, 512).transpose(0, 2, 1, 3).reshape(4, 128, 1024))

    def pairs(w):
        return np.ascontiguousarray(w.reshape(4, 128, 4, 2, 128).transpose(2, 1, 3, 0, 4).reshape(4, 128, 1024))

    def feature_major(v):
        return np.ascontiguousarray(v.T.reshape(8, 128, -1).transpose(1, 0, 2))

    vec = np.zeros((128, NV), f)

    def put(name, v):
        lo, hi = COL[name]
        vec[:v.shape[0], lo:hi] = v

    put("g_pre1", cols(x["attn_pre_norm"][0]))
    put("g_post1", cols(x["attn_post_norm"][0]))
    put("g_pre2", cols(x["ffn_pre_norm"][0]))
    put("g_post2", cols(x["ffn_post_norm"][0]))
    put("subln", cols(x["diff_subln"][0]))
    put("sbn", np.concatenate([x["sb_norm"][0]] * 2)[:, None])
    put("lam", np.stack([x["lambda_q1"][0], x["lambda_q2"][0], x["lambda_k1"][0], x["lambda_k2"][0]], axis=1))
    put("table", np.concatenate([x["rel_bias"], np.full((1, 4), NEG, f)]))
    put("sink", np.broadcast_to(x["sink_2"][0][None, :], (128, 8)))
    put("cw", cols(x["conv_w"][0]))
    put("cb", cols(x["conv_b"][0]))
    put("c", np.stack([cols(x["c_2"][0]), cols(x["c_ctx_2"])], axis=2).reshape(128, 16))
    put("bmod", cols(x["b_mod_2"][0]))
    for n, s in (("h_pre1", "g_pre1_2"), ("h_post1", "g_post1_2"), ("h_pre2", "g_pre2_2"), ("h_post2", "g_post2_2")):
        put(n, cols(x[s][0]))
    put("dw", cols(x["conv_w_2"][0]))
    put("db", cols(x["conv_b_2"][0]))
    put("sel", np.eye(2, dtype=f)[[0, 1, 0, 1]])

    consts, onehot, rope, dft = _shapes_only()
    qkv = x["w_qkv"][0]
    win = x["w_in_2"][0]
    heads = [0, 4, 1, 5, 2, 6, 3, 7]
    up, up2 = by_out(x["w_up"][0]), by_out(x["w_up_2"][0])
    alt = np.arange(44).reshape(2, 22).T.reshape(44)
    wkv = np.stack([by_out(win[:, 512:640])[0], by_out(win[:, 640:768])[0]])
    arrays = {
        "vec": vec, "consts": consts, "onehot": onehot, "rope": rope,
        "x": feature_major(x["x"][0]), "ctx": feature_major(x["ctx_2"][0]),
        "w_dq": by_out(qkv[:, 0:512]), "w_dk": by_out(qkv[:, 512:1024]), "w_dv": by_in(qkv[:, 1024:1536]),
        "w_sq": by_out(qkv[:, 1536:2048]), "w_sk": by_out(qkv[:, 2048:2560]), "w_sv": by_in(qkv[:, 2560:3072]),
        "w_mod": np.concatenate([by_in(x["w_mod_2"][0][:, 512 * i:512 * i + 512]) for i in range(12)]),
        "w_o": by_out(x["w_o"][0]),
        "w_up": up[alt], "w_down": x["w_down"][0].reshape(22, 128, 1024),
        "w_kv2": wkv, "w_q2": by_out(win[:, 0:512].reshape(1024, 8, 64)[:, heads].reshape(1024, 512)),
        "w_f2": by_out(win[:, 768:1280]), "w_g2": by_out(win[:, 1280:3328]), "w_dft": dft,
        "w_pa": pairs(x["w_pa_2"][0].reshape(8, 64, 1024)[heads].reshape(512, 1024)), "w_pf": pairs(x["w_pf_2"][0]),
        "w_out2": by_out(x["w_out_2"][0]), "w_up2": up2[alt], "w_down2": x["w_down_2"][0].reshape(22, 128, 1024),
    }
    nc = _bacc.Bacc("TRN2", target_bir_lowering=False, num_devices=1)
    aps, ins = {}, {}
    for name, v in arrays.items():
        v = np.ascontiguousarray(v)
        ins[f"in_{name}"] = v
        aps[name] = nc.dram_tensor(f"in_{name}", v.shape, mybir.dt.from_np(v.dtype), kind="ExternalInput").ap()
    aps["scratch"] = nc.dram_tensor("bias_rows", [128, 4, 640], mybir.dt.float32, kind="Internal").ap()
    o = nc.dram_tensor("out_x", [128, 8, 512], mybir.dt.float32, kind="ExternalOutput").ap()
    build(nc, aps, o)
    r = _run(nc, [ins], core_ids=[0])
    y = r.results[0]["out_x"]
    return np.ascontiguousarray(y.transpose(1, 0, 2).reshape(1024, 512).T)[None]
```
